# Optimizing a Trainium2 kernel written in Bass

```python
import math
import jax, jax.numpy as jnp
from jax import lax
import numpy as np

D_MODEL = 1024
BATCH = 1
SEQ = 256
DEPTH = 2

MLA_HEADS = 4
MLA_NOPE = 128
MLA_ROPE = 64
MLA_V = 128
MLA_Q_RANK = 384
MLA_KV_RANK = 256
ROPE_THETA = 10000.0
DIFF_HEADS = 4
DIFF_QK = 64
DIFF_V = 2 * DIFF_QK
MIX_WIDTH = MLA_HEADS * MLA_V + DIFF_HEADS * DIFF_V
IN_SIZES = (MLA_Q_RANK, MLA_KV_RANK, MLA_ROPE,
            DIFF_HEADS * 2 * DIFF_QK, DIFF_HEADS * 2 * DIFF_QK, DIFF_HEADS * DIFF_V)
IN_COLS = MLA_Q_RANK + MLA_KV_RANK + MLA_ROPE + 3 * DIFF_HEADS * 2 * DIFF_QK
NUM_BUCKETS = 32
MAX_DISTANCE = 128
D_FF_DENSE = 2816
N_EXPERTS = 8
TOP_K = 2
D_FF_EXPERT = 3584
N_DENSE = (DEPTH + 1) // 2
N_MOE = DEPTH // 2
DN_ALPHA = (2 * DEPTH) ** 0.25
DN_BETA = (8 * DEPTH) ** -0.25
BLOCK_Q = 128


def layer_norm(x, g, b, eps=1e-5):
    xf = x.astype(jnp.float32)
    mu = jnp.mean(xf, -1, keepdims=True)
    var = jnp.mean(jnp.square(xf - mu), -1, keepdims=True)
    return ((xf - mu) * lax.rsqrt(var + eps) * g.astype(jnp.float32) + b.astype(jnp.float32)).astype(x.dtype)

def rms_norm(x, g, eps):
    xf = x.astype(jnp.float32)
    return (xf * lax.rsqrt(jnp.mean(jnp.square(xf), -1, keepdims=True) + eps) * g.astype(jnp.float32)).astype(x.dtype)

def rope_tables(seq):
    pos = jnp.arange(seq, dtype=jnp.float32)
    inv = 1.0 / (ROPE_THETA ** (jnp.arange(0, MLA_ROPE, 2, dtype=jnp.float32) / MLA_ROPE))
    ang = pos[:, None] * inv[None, :]
    return jnp.cos(ang), jnp.sin(ang)

def apply_rope(x, cos, sin):
    xf = x.astype(jnp.float32)
    x1, x2 = jnp.split(xf, 2, axis=-1)
    return jnp.concatenate([x1 * cos - x2 * sin, x2 * cos + x1 * sin], -1).astype(x.dtype)

def t5_causal_bucket(n):
    max_exact = NUM_BUCKETS // 2
    nf = jnp.maximum(n, 1).astype(jnp.float32)
    large = max_exact + (jnp.log(nf / max_exact) / math.log(MAX_DISTANCE / max_exact)
                         * (NUM_BUCKETS - max_exact)).astype(jnp.int32)
    large = jnp.minimum(large, NUM_BUCKETS - 1)
    return jnp.where(n < max_exact, n, large)

def _block_positions(q0, seq):
    qpos = q0 + jnp.arange(BLOCK_Q)
    kpos = jnp.arange(seq)
    return qpos, kpos, kpos[None, :] <= qpos[:, None]

def mla_attention(q_nope, q_rope, k_nope, k_rope, v):
    b, s, h, dv = v.shape
    scale = (MLA_NOPE + MLA_ROPE) ** -0.5

    def block(q0):
        qn = lax.dynamic_slice_in_dim(q_nope, q0, BLOCK_Q, 1)
        qr = lax.dynamic_slice_in_dim(q_rope, q0, BLOCK_Q, 1)
        logits = (jnp.einsum('bqhd,bkhd->bhqk', qn, k_nope).astype(jnp.float32)
                  + jnp.einsum('bqhd,bkd->bhqk', qr, k_rope).astype(jnp.float32)) * scale
        _, _, mask = _block_positions(q0, s)
        p = jax.nn.softmax(jnp.where(mask, logits, -jnp.inf), axis=-1).astype(v.dtype)
        return jnp.einsum('bhqk,bkhd->bqhd', p, v)

    out = lax.map(block, jnp.arange(s // BLOCK_Q) * BLOCK_Q)
    return jnp.moveaxis(out, 0, 1).reshape(b, s, h, dv)

def diff_attention(q, k, v, bias_dist, lam):
    b, s, h, dv = v.shape
    scale = DIFF_QK ** -0.5

    def block(q0):
        qb = lax.dynamic_slice_in_dim(q, q0, BLOCK_Q, 1)
        logits = jnp.einsum('bqhcd,bkhcd->bhcqk', qb, k).astype(jnp.float32) * scale
        qpos, kpos, mask = _block_positions(q0, s)
        rel = jnp.maximum(qpos[:, None] - kpos[None, :], 0)
        bias = jnp.transpose(bias_dist[rel], (2, 0, 1))
        logits = jnp.where(mask, logits + bias[None, :, None], -jnp.inf)
        p = jax.nn.softmax(logits, axis=-1)
        a = (p[:, :, 0] - lam * p[:, :, 1]).astype(v.dtype)
        return jnp.einsum('bhqk,bkhd->bqhd', a, v)

    out = lax.map(block, jnp.arange(s // BLOCK_Q) * BLOCK_Q)
    return jnp.moveaxis(out, 0, 1).reshape(b, s, h, dv)

def hybrid_mixer(x, w_in, q_norm, kv_norm, w_uq, w_uk, w_uv, lam_params, diff_norm, w_o,
                 cos, sin, bias_dist, lambda_init):
    b, s, _ = x.shape
    h = x @ w_in
    splits, acc = [], 0
    for size in IN_SIZES[:-1]:
        acc += size
        splits.append(acc)
    c_q, c_kv, k_r, dq, dk, dv = jnp.split(h, splits, axis=-1)

    q = (rms_norm(c_q, q_norm, 1e-6) @ w_uq).reshape(b, s, MLA_HEADS, MLA_NOPE + MLA_ROPE)
    q_nope = q[..., :MLA_NOPE]
    q_rope = apply_rope(q[..., MLA_NOPE:], cos[None, :, None], sin[None, :, None])
    c_kv = rms_norm(c_kv, kv_norm, 1e-6)
    k_nope = (c_kv @ w_uk).reshape(b, s, MLA_HEADS, MLA_NOPE)
    v_mla = (c_kv @ w_uv).reshape(b, s, MLA_HEADS, MLA_V)
    k_rope = apply_rope(k_r, cos[None], sin[None])
    mla_out = mla_attention(q_nope, q_rope, k_nope, k_rope, v_mla).reshape(b, s, MLA_HEADS * MLA_V)

    lp = lam_params.astype(jnp.float32)
    lam = jnp.exp(jnp.sum(lp[0] * lp[1])) - jnp.exp(jnp.sum(lp[2] * lp[3])) + lambda_init
    dq = dq.reshape(b, s, DIFF_HEADS, 2, DIFF_QK)
    dk = dk.reshape(b, s, DIFF_HEADS, 2, DIFF_QK)
    dv = dv.reshape(b, s, DIFF_HEADS, DIFF_V)
    d_out = diff_attention(dq, dk, dv, bias_dist, lam)
    d_out = rms_norm(d_out, diff_norm, 1e-5) * (1.0 - lambda_init)

    merged = jnp.concatenate([mla_out, d_out.reshape(b, s, DIFF_HEADS * DIFF_V)], axis=-1)
    return merged @ w_o

def swiglu(x, wg, wu, wd):
    return (jax.nn.silu(x @ wg) * (x @ wu)) @ wd

def moe_swiglu(x, router, wg, wu, wd):
    b, s, d = x.shape
    xf = x.reshape(b * s, d)
    logits = (xf @ router).astype(jnp.float32)
    top_v, top_i = lax.top_k(logits, TOP_K)
    gates = jax.nn.softmax(top_v, axis=-1)
    dense_g = jnp.sum(jax.nn.one_hot(top_i, N_EXPERTS, dtype=jnp.float32) * gates[..., None], axis=1).astype(x.dtype)
    y = jnp.zeros_like(xf)
    for e in range(N_EXPERTS):
        y = y + dense_g[:, e:e + 1] * swiglu(xf, wg[e], wu[e], wd[e])
    return y.reshape(b, s, d)

def first_inputs(seed: int = 0) -> dict:
    key = jax.random.key(seed)
    ks = jax.random.split(key, 24)

    def nrm(k, shape, scale):
        return jax.random.normal(k, shape, jnp.float32) * scale

    col_scale = jnp.concatenate([jnp.ones((IN_COLS - DIFF_HEADS * DIFF_V,), jnp.float32),
                                 jnp.full((DIFF_HEADS * DIFF_V,), DN_BETA, jnp.float32)])
    return {
        "x": nrm(ks[0], (BATCH, SEQ, D_MODEL), 1.0),
        "rel_bias": nrm(ks[1], (NUM_BUCKETS, DIFF_HEADS), 0.5),
        "w_in": nrm(ks[2], (DEPTH, D_MODEL, IN_COLS), D_MODEL ** -0.5) * col_scale,
        "mla_q_norm": 1.0 + nrm(ks[3], (DEPTH, MLA_Q_RANK), 0.02),
        "mla_kv_norm": 1.0 + nrm(ks[4], (DEPTH, MLA_KV_RANK), 0.02),
        "mla_w_uq": nrm(ks[5], (DEPTH, MLA_Q_RANK, MLA_HEADS * (MLA_NOPE + MLA_ROPE)), MLA_Q_RANK ** -0.5),
        "mla_w_uk": nrm(ks[6], (DEPTH, MLA_KV_RANK, MLA_HEADS * MLA_NOPE), MLA_KV_RANK ** -0.5),
        "mla_w_uv": nrm(ks[7], (DEPTH, MLA_KV_RANK, MLA_HEADS * MLA_V), MLA_KV_RANK ** -0.5 * DN_BETA),
        "diff_lambda": nrm(ks[8], (DEPTH, 4, DIFF_QK), 0.1),
        "diff_norm": 1.0 + nrm(ks[9], (DEPTH, DIFF_V), 0.02),
        "w_o": nrm(ks[10], (DEPTH, MIX_WIDTH, D_MODEL), MIX_WIDTH ** -0.5 * DN_BETA),
        "ln1_g": 1.0 + nrm(ks[11], (DEPTH, D_MODEL), 0.02),
        "ln1_b": nrm(ks[12], (DEPTH, D_MODEL), 0.02),
        "ln2_g": 1.0 + nrm(ks[13], (DEPTH, D_MODEL), 0.02),
        "ln2_b": nrm(ks[14], (DEPTH, D_MODEL), 0.02),
        "ffn_w_gate": nrm(ks[15], (N_DENSE, D_MODEL, D_FF_DENSE), D_MODEL ** -0.5 * DN_BETA),
        "ffn_w_up": nrm(ks[16], (N_DENSE, D_MODEL, D_FF_DENSE), D_MODEL ** -0.5 * DN_BETA),
        "ffn_w_down": nrm(ks[17], (N_DENSE, D_FF_DENSE, D_MODEL), D_FF_DENSE ** -0.5 * DN_BETA),
        "moe_router": nrm(ks[18], (N_MOE, D_MODEL, N_EXPERTS), D_MODEL ** -0.5),
        "moe_w_gate": nrm(ks[19], (N_MOE, N_EXPERTS, D_MODEL, D_FF_EXPERT), D_MODEL ** -0.5 * DN_BETA),
        "moe_w_up": nrm(ks[20], (N_MOE, N_EXPERTS, D_MODEL, D_FF_EXPERT), D_MODEL ** -0.5 * DN_BETA),
        "moe_w_down": nrm(ks[21], (N_MOE, N_EXPERTS, D_FF_EXPERT, D_MODEL), D_FF_EXPERT ** -0.5 * DN_BETA),
    }

def first_block(x, rel_bias, w_in, mla_q_norm, mla_kv_norm, mla_w_uq, mla_w_uk, mla_w_uv,
              diff_lambda, diff_norm, w_o, ln1_g, ln1_b, ln2_g, ln2_b,
              ffn_w_gate, ffn_w_up, ffn_w_down, moe_router, moe_w_gate, moe_w_up, moe_w_down):
    seq = x.shape[1]
    cos, sin = rope_tables(seq)
    bias_dist = rel_bias.astype(jnp.float32)[t5_causal_bucket(jnp.arange(seq))]
    for l in range(DEPTH):
        lambda_init = 0.8 - 0.6 * math.exp(-0.3 * l)
        mix = hybrid_mixer(x, w_in[l], mla_q_norm[l], mla_kv_norm[l], mla_w_uq[l], mla_w_uk[l],
                           mla_w_uv[l], diff_lambda[l], diff_norm[l], w_o[l],
                           cos, sin, bias_dist, lambda_init)
        x = layer_norm(DN_ALPHA * x + mix, ln1_g[l], ln1_b[l])
        if l % 2 == 0:
            f = swiglu(x, ffn_w_gate[l // 2], ffn_w_up[l // 2], ffn_w_down[l // 2])
        else:
            f = moe_swiglu(x, moe_router[l // 2], moe_w_gate[l // 2], moe_w_up[l // 2], moe_w_down[l // 2])
        x = layer_norm(DN_ALPHA * x + f, ln2_g[l], ln2_b[l])
    return x


PLE_DIM = 256
N_EVEN = (DEPTH + 1) // 2
N_ODD = DEPTH // 2
RG_WIDTH = 512
RG_BLOCKS = 8
RG_BLOCK = RG_WIDTH // RG_BLOCKS
RG_CONV = 4
RG_C = 8.0
ML_HEADS = 4
ML_HEAD_DIM = 128
ML_WIDTH = ML_HEADS * ML_HEAD_DIM
ML_CONV = 4
ML_CHUNK = 64
HY_IN = 2 * RG_WIDTH + 4 * ML_WIDTH + 2 * ML_HEADS
HY_MIX = RG_WIDTH + ML_WIDTH
AT_HEADS = 16
AT_KV_HEADS = 4
AT_HEAD_DIM = 64
WINDOW = 128
AT_QKV = (AT_HEADS + 2 * AT_KV_HEADS) * AT_HEAD_DIM
FF_DIM = 3 * D_MODEL
FF_CONV = 3
EPS = 1e-6


def rms_norm_2(x, g):
    xf = x.astype(jnp.float32)
    y = xf * lax.rsqrt(jnp.mean(xf * xf, axis=-1, keepdims=True) + EPS)
    return (y * g.astype(jnp.float32)).astype(x.dtype)

def causal_dwconv(x, w, b):
    k_w = w.shape[0]
    s = x.shape[1]
    xp = jnp.pad(x, ((0, 0), (k_w - 1, 0), (0, 0)))
    y = xp[:, 0:s] * w[0]
    for j in range(1, k_w):
        y = y + xp[:, j:j + s] * w[j]
    return y + b

def _linear_recurrence_combine(left, right):
    a_l, b_l = left
    a_r, b_r = right
    return a_l * a_r, a_r * b_l + b_r

def rg_lru(x, w_a, b_a, w_x, b_x, lam):
    f32 = jnp.float32
    bsz, s, _ = x.shape
    xf = x.astype(f32)
    xb = xf.reshape(bsz, s, RG_BLOCKS, RG_BLOCK)
    r = jax.nn.sigmoid(jnp.einsum('bsni,nij->bsnj', xb, w_a.astype(f32)).reshape(bsz, s, RG_WIDTH) + b_a.astype(f32))
    i = jax.nn.sigmoid(jnp.einsum('bsni,nij->bsnj', xb, w_x.astype(f32)).reshape(bsz, s, RG_WIDTH) + b_x.astype(f32))
    log_a = -RG_C * r * jax.nn.softplus(-lam.astype(f32))
    a = jnp.exp(log_a)
    u = jnp.sqrt(-jnp.expm1(2.0 * log_a)) * (i * xf)
    _, h = lax.associative_scan(_linear_recurrence_combine, (a, u), axis=1)
    return h

def mlstm_chunkwise(q, k, v, i_pre, f_pre):
    f32 = jnp.float32
    bsz, s, nh, dh = q.shape
    nc = s // ML_CHUNK

    def to_chunks(t):
        return t.astype(f32).reshape(bsz, nc, ML_CHUNK, nh, dh).transpose(0, 3, 1, 2, 4)

    def gate_chunks(t):
        return t.astype(f32).reshape(bsz, nc, ML_CHUNK, nh).transpose(0, 3, 1, 2)

    qc = to_chunks(q)
    kc = to_chunks(k) * (dh ** -0.5)
    vc = to_chunks(v)
    log_i = gate_chunks(i_pre)
    log_f = jax.nn.log_sigmoid(gate_chunks(f_pre))
    b = jnp.cumsum(log_f, axis=-1)
    b_last = b[..., -1]

    g = b_last[..., None] - b + log_i
    m_loc = jnp.max(g, axis=-1)
    w_loc = jnp.exp(g - m_loc[..., None])
    c_loc = jnp.einsum('bhcl,bhcld,bhcle->bhcde', w_loc, kc, vc)
    n_loc = jnp.einsum('bhcl,bhcld->bhcd', w_loc, kc)

    def step(carry, inp):
        c_st, n_st, m_st = carry
        c_l, n_l, m_l, b_l = inp
        m_new = jnp.maximum(b_l + m_st, m_l)
        a_prev = jnp.exp(b_l + m_st - m_new)
        a_loc = jnp.exp(m_l - m_new)
        c_new = a_prev[..., None, None] * c_st + a_loc[..., None, None] * c_l
        n_new = a_prev[..., None] * n_st + a_loc[..., None] * n_l
        return (c_new, n_new, m_new), (c_st, n_st, m_st)

    init = (jnp.zeros((bsz, nh, dh, dh), f32), jnp.zeros((bsz, nh, dh), f32), jnp.full((bsz, nh), -jnp.inf, f32))
    xs = (jnp.moveaxis(c_loc, 2, 0), jnp.moveaxis(n_loc, 2, 0), jnp.moveaxis(m_loc, 2, 0), jnp.moveaxis(b_last, 2, 0))
    _, (c_prev, n_prev, m_prev) = lax.scan(step, init, xs)
    c_prev = jnp.moveaxis(c_prev, 0, 2)
    n_prev = jnp.moveaxis(n_prev, 0, 2)
    m_prev = jnp.moveaxis(m_prev, 0, 2)

    idx = jnp.arange(ML_CHUNK)
    causal = idx[:, None] >= idx[None, :]
    d_log = b[..., :, None] - b[..., None, :] + log_i[..., None, :]
    d_log = jnp.where(causal, d_log, -jnp.inf)
    inter_log = b + m_prev[..., None]
    m_t = jnp.maximum(inter_log, jnp.max(d_log, axis=-1))
    w_intra = jnp.exp(d_log - m_t[..., None])
    a_inter = jnp.exp(inter_log - m_t)
    s_qk = jnp.einsum('bhctd,bhcsd->bhcts', qc, kc) * w_intra
    num = jnp.einsum('bhcts,bhcse->bhcte', s_qk, vc) + a_inter[..., None] * jnp.einsum('bhctd,bhcde->bhcte', qc, c_prev)
    den = jnp.sum(s_qk, axis=-1) + a_inter * jnp.einsum('bhctd,bhcd->bhct', qc, n_prev)
    h = num / jnp.maximum(jnp.abs(den), jnp.exp(-m_t))[..., None]
    return h.transpose(0, 2, 3, 1, 4).reshape(bsz, s, nh, dh)

def rglru_mlstm_mixer(h, w_in, b_in, rg_conv_w, rg_conv_b, rg_w_a, rg_b_a, rg_w_x, rg_b_x, rg_lambda,
                      ml_conv_w, ml_conv_b, ml_norm, w_out):
    f32 = jnp.float32
    bsz, s, _ = h.shape
    z = h @ w_in + b_in
    cuts = [RG_WIDTH, 2 * RG_WIDTH, 2 * RG_WIDTH + ML_WIDTH, 2 * RG_WIDTH + 2 * ML_WIDTH,
            2 * RG_WIDTH + 3 * ML_WIDTH, 2 * RG_WIDTH + 4 * ML_WIDTH, 2 * RG_WIDTH + 4 * ML_WIDTH + ML_HEADS]
    x_rg, g_rg, q, k, v, o, i_pre, f_pre = jnp.split(z, cuts, axis=-1)
    xc = causal_dwconv(x_rg, rg_conv_w, rg_conv_b)
    y_rg = rg_lru(xc, rg_w_a, rg_b_a, rg_w_x, rg_b_x, rg_lambda) * jax.nn.gelu(g_rg.astype(f32), approximate=True)
    qk = jax.nn.silu(causal_dwconv(jnp.concatenate([q, k], axis=-1), ml_conv_w, ml_conv_b))
    q, k = jnp.split(qk, 2, axis=-1)
    hm = mlstm_chunkwise(q.reshape(bsz, s, ML_HEADS, ML_HEAD_DIM), k.reshape(bsz, s, ML_HEADS, ML_HEAD_DIM),
                         v.reshape(bsz, s, ML_HEADS, ML_HEAD_DIM), i_pre, f_pre)
    hm = rms_norm_2(hm, ml_norm.reshape(ML_HEADS, ML_HEAD_DIM))
    y_ml = jax.nn.sigmoid(o.astype(f32)) * hm.reshape(bsz, s, ML_WIDTH)
    y = jnp.concatenate([y_rg, y_ml], axis=-1).astype(h.dtype)
    return y @ w_out

def rope_tables_2(positions):
    half = AT_HEAD_DIM // 2
    inv_freq = ROPE_THETA ** (-jnp.arange(half, dtype=jnp.float32) * (2.0 / AT_HEAD_DIM))
    ang = positions.astype(jnp.float32)[..., None] * inv_freq
    return jnp.cos(ang)[:, :, None, :], jnp.sin(ang)[:, :, None, :]

def apply_rope_2(x, cos, sin):
    xf = x.astype(jnp.float32)
    x1, x2 = jnp.split(xf, 2, axis=-1)
    return jnp.concatenate([x1 * cos - x2 * sin, x2 * cos + x1 * sin], axis=-1)

def banded_sink_attention(q, k, v, sinks):
    f32 = jnp.float32
    bsz, s, _, dh = q.shape
    nb = s // WINDOW
    grp = AT_HEADS // AT_KV_HEADS
    qb = q.astype(f32).reshape(bsz, nb, WINDOW, AT_KV_HEADS, grp, dh)

    def key_window(t):
        tb = t.astype(f32).reshape(bsz, nb, WINDOW, AT_KV_HEADS, dh)
        prev = jnp.pad(tb, ((0, 0), (1, 0), (0, 0), (0, 0), (0, 0)))[:, :-1]
        return jnp.concatenate([prev, tb], axis=2)

    kw = key_window(k)
    vw = key_window(v)
    logits = jnp.einsum('bnqhgd,bnkhd->bnhgqk', qb, kw) * (dh ** -0.5)
    qi = jnp.arange(WINDOW)[:, None]
    kj = jnp.arange(2 * WINDOW)[None, :]
    band = (kj > qi) & (kj <= qi + WINDOW)
    blk = jnp.arange(nb)[:, None, None]
    valid = band[None] & ((blk > 0) | (kj >= WINDOW)[None])
    logits = jnp.where(valid[None, :, None, None], logits, -jnp.inf)
    sink = sinks.astype(f32).reshape(AT_KV_HEADS, grp)[:, :, None]
    m = jnp.maximum(jnp.max(logits, axis=-1), sink)
    probs = jnp.exp(logits - m[..., None])
    denom = jnp.sum(probs, axis=-1) + jnp.exp(sink - m)
    out = jnp.einsum('bnhgqk,bnkhd->bnhgqd', probs, vw) / denom[..., None]
    return out.transpose(0, 1, 4, 2, 3, 5).reshape(bsz, s, AT_HEADS * dh)

def swa_sink_mixer(h, positions, w_qkv, q_norm, k_norm, sinks, w_out):
    bsz, s, _ = h.shape
    qkv = h @ w_qkv
    q, k, v = jnp.split(qkv, [AT_HEADS * AT_HEAD_DIM, (AT_HEADS + AT_KV_HEADS) * AT_HEAD_DIM], axis=-1)
    q = q.reshape(bsz, s, AT_HEADS, AT_HEAD_DIM)
    k = k.reshape(bsz, s, AT_KV_HEADS, AT_HEAD_DIM)
    v = v.reshape(bsz, s, AT_KV_HEADS, AT_HEAD_DIM)
    cos, sin = rope_tables_2(positions)
    q = apply_rope_2(rms_norm_2(q, q_norm), cos, sin)
    k = apply_rope_2(rms_norm_2(k, k_norm), cos, sin)
    o = banded_sink_attention(q, k, v, sinks)
    return o.astype(h.dtype) @ w_out

def conv_ffn(h, w_up, conv_w, conv_b, w_down):
    g, u = jnp.split(h @ w_up, 2, axis=-1)
    g = causal_dwconv(g, conv_w, conv_b)
    return (jax.nn.gelu(g, approximate=True) * u) @ w_down

def _normal(key, shape, scale):
    return jax.random.normal(key, shape, jnp.float32) * scale

def second_inputs(seed: int = 0) -> dict:
    key = jax.random.key(seed)
    ks = jax.random.split(key, 30)
    x = _normal(ks[0], (BATCH, SEQ, D_MODEL), 1.0)
    p = _normal(ks[1], (DEPTH, BATCH, SEQ, PLE_DIM), 1.0)
    offs = jax.random.randint(ks[2], (BATCH, 1), 0, 1024, dtype=jnp.int32)
    positions = offs + jnp.arange(SEQ, dtype=jnp.int32)[None, :]
    norm_mix = 1.0 + _normal(ks[3], (DEPTH, D_MODEL), 0.05)
    norm_ffn = 1.0 + _normal(ks[4], (DEPTH, D_MODEL), 0.05)
    norm_ple = 1.0 + _normal(ks[5], (DEPTH, D_MODEL), 0.05)
    hy_w_in = _normal(ks[6], (N_EVEN, D_MODEL, HY_IN), D_MODEL ** -0.5)
    hy_b_in = _normal(ks[7], (N_EVEN, HY_IN), 0.02)
    hy_b_in = hy_b_in.at[:, HY_IN - ML_HEADS:].add(jnp.linspace(3.0, 6.0, ML_HEADS))
    rg_conv_w = _normal(ks[8], (N_EVEN, RG_CONV, RG_WIDTH), RG_CONV ** -0.5)
    rg_conv_b = _normal(ks[9], (N_EVEN, RG_WIDTH), 0.02)
    rg_w_a = _normal(ks[10], (N_EVEN, RG_BLOCKS, RG_BLOCK, RG_BLOCK), RG_BLOCK ** -0.5)
    rg_b_a = _normal(ks[11], (N_EVEN, RG_WIDTH), 0.02)
    rg_w_x = _normal(ks[12], (N_EVEN, RG_BLOCKS, RG_BLOCK, RG_BLOCK), RG_BLOCK ** -0.5)
    rg_b_x = _normal(ks[13], (N_EVEN, RG_WIDTH), 0.02)
    a_c = jax.random.uniform(ks[14], (N_EVEN, RG_WIDTH), jnp.float32, 0.9, 0.999)
    a_base = a_c ** (1.0 / RG_C)
    rg_lambda = jnp.log(a_base) - jnp.log1p(-a_base)
    ml_conv_w = _normal(ks[15], (N_EVEN, ML_CONV, 2 * ML_WIDTH), ML_CONV ** -0.5)
    ml_conv_b = _normal(ks[16], (N_EVEN, 2 * ML_WIDTH), 0.02)
    ml_norm = 1.0 + _normal(ks[17], (N_EVEN, ML_WIDTH), 0.05)
    hy_w_out = _normal(ks[18], (N_EVEN, HY_MIX, D_MODEL), HY_MIX ** -0.5)
    at_w_qkv = _normal(ks[19], (N_ODD, D_MODEL, AT_QKV), D_MODEL ** -0.5)
    at_q_norm = 1.0 + _normal(ks[20], (N_ODD, AT_HEAD_DIM), 0.05)
    at_k_norm = 1.0 + _normal(ks[21], (N_ODD, AT_HEAD_DIM), 0.05)
    at_sinks = _normal(ks[22], (N_ODD, AT_HEADS), 0.5)
    at_w_out = _normal(ks[23], (N_ODD, AT_HEADS * AT_HEAD_DIM, D_MODEL), (AT_HEADS * AT_HEAD_DIM) ** -0.5)
    ff_w_up = _normal(ks[24], (DEPTH, D_MODEL, 2 * FF_DIM), D_MODEL ** -0.5)
    ff_conv_w = _normal(ks[25], (DEPTH, FF_CONV, FF_DIM), FF_CONV ** -0.5)
    ff_conv_b = _normal(ks[26], (DEPTH, FF_DIM), 0.02)
    ff_w_down = _normal(ks[27], (DEPTH, FF_DIM, D_MODEL), FF_DIM ** -0.5)
    ple_w_gate = _normal(ks[28], (DEPTH, D_MODEL, D_MODEL), D_MODEL ** -0.5)
    ple_w_proj = _normal(ks[29], (DEPTH, PLE_DIM, D_MODEL), PLE_DIM ** -0.5)
    return {'x': x, 'p': p, 'positions': positions,
            'norm_mix': norm_mix, 'norm_ffn': norm_ffn, 'norm_ple': norm_ple,
            'hy_w_in': hy_w_in, 'hy_b_in': hy_b_in,
            'rg_conv_w': rg_conv_w, 'rg_conv_b': rg_conv_b, 'rg_w_a': rg_w_a, 'rg_b_a': rg_b_a,
            'rg_w_x': rg_w_x, 'rg_b_x': rg_b_x, 'rg_lambda': rg_lambda,
            'ml_conv_w': ml_conv_w, 'ml_conv_b': ml_conv_b, 'ml_norm': ml_norm, 'hy_w_out': hy_w_out,
            'at_w_qkv': at_w_qkv, 'at_q_norm': at_q_norm, 'at_k_norm': at_k_norm, 'at_sinks': at_sinks,
            'at_w_out': at_w_out,
            'ff_w_up': ff_w_up, 'ff_conv_w': ff_conv_w, 'ff_conv_b': ff_conv_b, 'ff_w_down': ff_w_down,
            'ple_w_gate': ple_w_gate, 'ple_w_proj': ple_w_proj}

def second_block(x, p, positions, norm_mix, norm_ffn, norm_ple, hy_w_in, hy_b_in,
              rg_conv_w, rg_conv_b, rg_w_a, rg_b_a, rg_w_x, rg_b_x, rg_lambda,
              ml_conv_w, ml_conv_b, ml_norm, hy_w_out,
              at_w_qkv, at_q_norm, at_k_norm, at_sinks, at_w_out,
              ff_w_up, ff_conv_w, ff_conv_b, ff_w_down, ple_w_gate, ple_w_proj):
    for layer in range(DEPTH):
        h = rms_norm_2(x, norm_mix[layer])
        if layer % 2 == 0:
            e = layer // 2
            mix = rglru_mlstm_mixer(h, hy_w_in[e], hy_b_in[e], rg_conv_w[e], rg_conv_b[e], rg_w_a[e], rg_b_a[e],
                                    rg_w_x[e], rg_b_x[e], rg_lambda[e], ml_conv_w[e], ml_conv_b[e], ml_norm[e],
                                    hy_w_out[e])
        else:
            o = layer // 2
            mix = swa_sink_mixer(h, positions, at_w_qkv[o], at_q_norm[o], at_k_norm[o], at_sinks[o], at_w_out[o])
        x = x + mix.astype(x.dtype)
        x = x + conv_ffn(rms_norm_2(x, norm_ffn[layer]), ff_w_up[layer], ff_conv_w[layer], ff_conv_b[layer],
                         ff_w_down[layer]).astype(x.dtype)
        gate = jax.nn.sigmoid(rms_norm_2(x, norm_ple[layer]) @ ple_w_gate[layer])
        x = x + (gate * (p[layer] @ ple_w_proj[layer])).astype(x.dtype)
    return x


def setup_inputs(seed=0):
    out = dict(first_inputs(seed))
    for name, value in second_inputs(seed + 1).items():
        if name != "x":
            out[name + "_2"] = value
    return out


def reference(
    x, rel_bias, w_in, mla_q_norm, mla_kv_norm, mla_w_uq, mla_w_uk, mla_w_uv, diff_lambda,
    diff_norm, w_o, ln1_g, ln1_b, ln2_g, ln2_b, ffn_w_gate, ffn_w_up, ffn_w_down, moe_router,
    moe_w_gate, moe_w_up, moe_w_down, p_2, positions_2, norm_mix_2, norm_ffn_2, norm_ple_2,
    hy_w_in_2, hy_b_in_2, rg_conv_w_2, rg_conv_b_2, rg_w_a_2, rg_b_a_2, rg_w_x_2, rg_b_x_2,
    rg_lambda_2, ml_conv_w_2, ml_conv_b_2, ml_norm_2, hy_w_out_2, at_w_qkv_2, at_q_norm_2,
    at_k_norm_2, at_sinks_2, at_w_out_2, ff_w_up_2, ff_conv_w_2, ff_conv_b_2, ff_w_down_2,
    ple_w_gate_2, ple_w_proj_2,
):
    x = first_block(
        x, rel_bias, w_in, mla_q_norm, mla_kv_norm, mla_w_uq, mla_w_uk, mla_w_uv, diff_lambda,
        diff_norm, w_o, ln1_g, ln1_b, ln2_g, ln2_b, ffn_w_gate, ffn_w_up, ffn_w_down,
        moe_router, moe_w_gate, moe_w_up, moe_w_down,
    )
    return second_block(
        x, p_2, positions_2, norm_mix_2, norm_ffn_2, norm_ple_2, hy_w_in_2, hy_b_in_2,
        rg_conv_w_2, rg_conv_b_2, rg_w_a_2, rg_b_a_2, rg_w_x_2, rg_b_x_2, rg_lambda_2,
        ml_conv_w_2, ml_conv_b_2, ml_norm_2, hy_w_out_2, at_w_qkv_2, at_q_norm_2, at_k_norm_2,
        at_sinks_2, at_w_out_2, ff_w_up_2, ff_conv_w_2, ff_conv_b_2, ff_w_down_2, ple_w_gate_2,
        ple_w_proj_2,
    )


_drawn_inputs = setup_inputs


def setup_inputs(seed=0):
    import zlib

    import numpy as np

    out = dict(_drawn_inputs(seed))
    spreads = {}
    factors = {'mla_q_norm': 8.0,
     'mla_kv_norm': 8.0,
     'diff_lambda': 2.745,
     'diff_norm': 6.262,
     'norm_ple_2': 5.795,
     'rg_b_a_2': 8.0,
     'rg_b_x_2': 8.0,
     'ml_conv_b_2': 7.6,
     'at_q_norm_2': 8.0,
     'at_k_norm_2': 8.0,
     'at_sinks_2': 52.279,
     'ff_conv_b_2': 4.494}
    for name, (base, spread) in spreads.items():
        noise = np.random.default_rng([zlib.crc32(name.encode()), seed]).standard_normal(out[name].shape)
        drawn = base * np.exp(spread * noise) if base else spread * noise
        out[name] = __import__('jax').numpy.asarray(drawn.astype(out[name].dtype))
    for name, factor in factors.items():
        out[name] = (out[name] * factor).astype(out[name].dtype)
    return out
```

```python
import math
from contextlib import ExitStack

import numpy as np
import concourse.bass as bass
from concourse import mybir

ALU = mybir.AluOpType
ACT = mybir.ActivationFunctionType
F = mybir.dt.float32
I32 = mybir.dt.int32
AX = mybir.AxisListType.X
P = 128
STOP = 99
CAP = 128
NS = 4
NEG = -1e30
ALPHA = 4 ** 0.25
HEAD = [0, 2, 1, 3]
GELU_C = math.sqrt(2.0 / math.pi)

CONSTS = [("ident", 128), ("ones", 256), ("tri", 128), ("iota", 256), ("bd2", 2), ("rot", 128), ("anti", 128), ("fold", 128),
          ("maskM", 256), ("maskW", 256), ("cos1", 256), ("oh", 384), ("sel4", 512), ("tri8", 64), ("invf", 1)]
SMALLS = [("qn0", 3), ("qn1", 3), ("kvn0", 2), ("kvn1", 2), ("dn0", 1), ("dn1", 1),
          ("g10", 8), ("g11", 8), ("b10", 8), ("b11", 8), ("g20", 8), ("g21", 8), ("b20", 8), ("b21", 8),
          ("router", 64), ("nm0", 8), ("nm1", 8), ("nf0", 8), ("nf1", 8), ("np0", 8), ("np1", 8),
          ("bin", 24), ("bif", 2), ("wif", 64), ("rcw", 16), ("rcb", 4), ("rwa", 256), ("rwx", 256), ("rba", 4), ("rbx", 4),
          ("lam", 4), ("mcw", 32), ("mcb", 8), ("mnorm", 4), ("aqn", 1), ("akn", 1), ("sinks", 16),
          ("fcw0", 72), ("fcw1", 72), ("fcb0", 24), ("fcb1", 24), ("dl0", 4), ("dl1", 4), ("relb", 4)]


def offsets(table):
    at, out = 0, {}
    for name, n in table:
        out[name] = (at, n)
        at += n
    return out, at


def const_array():
    off, total = offsets(CONSTS)
    c = np.zeros((P, total), np.float32)

    def put(name, v):
        a, n = off[name]
        v = np.asarray(v, np.float32)
        c[:v.shape[0], a:a + n] = v

    p = np.arange(P)[:, None]
    f = np.arange(P)[None, :]
    put("ident", np.eye(P))
    put("ones", np.ones((P, 256)))
    put("tri", p < f)
    put("iota", np.tile(np.arange(256), (P, 1)))
    put("bd2", np.concatenate([p < 64, p >= 64], 1))
    d = np.arange(P)
    r = np.zeros((P, P))
    for j in range(P):
        if j % 64 < 32:
            r[j + 32, j] = -1
        else:
            r[j - 32, j] = 1
    put("rot", r)
    put("anti", p + f == P - 1)
    put("fold", (p % 64) == (f % 64))
    j = np.arange(256)[None, :]
    put("maskM", np.where(j <= 128 + p, 0.0, NEG))
    put("maskW", np.where((j <= 128 + p) & (j > p), 0.0, NEG))
    pos = np.arange(256, dtype=np.float32)
    inv = (np.float32(1.0) / (np.float32(10000.0) ** (np.arange(0, 64, 2, dtype=np.float32) / np.float32(64)))).astype(np.float32)
    ang = (pos[:, None] * inv[None, :]).astype(np.float32)
    cs, sn = np.cos(ang).T, np.sin(ang).T
    put("cos1", np.concatenate([cs, cs, -sn, sn], 0))
    n = np.arange(256)
    nf = np.maximum(n, 1).astype(np.float32)
    large = 16 + (np.log(nf / np.float32(16)) / np.float32(math.log(8.0)) * np.float32(16)).astype(np.int32)
    bucket = np.where(n < 16, n, np.minimum(large, 31))
    oh = np.zeros((32, 384))
    oh[bucket, 255 - n] = 1
    put("oh", oh)
    s4 = np.zeros((4, 4, P))
    for h in range(4):
        s4[h, h] = 1
    put("sel4", s4.reshape(4, 512))
    put("tri8", np.tile((np.arange(8)[None, :] < np.arange(8)[:, None]).reshape(1, 64), (P, 1)))
    half = np.float32(10000.0) ** (-np.arange(32, dtype=np.float32) * np.float32(2.0 / 64))
    put("invf", half.astype(np.float32)[d % 32][:, None])
    return c


class Prog:

    def __init__(self, nc, ctx):
        self.nc, self.ctx = nc, ctx
        self.q = {e: [] for e in "TVAGS"}
        self.known = {e: {} for e in "TVAGS"}
        self.count = {}
        self.own = {}
        self.fresh("")

    def sem(self, name):
        s = self.ctx.enter_context(self.nc.semaphore(name))
        self.count[s] = 0
        return s

    def fresh(self, tag):
        self.own = {e: self.sem(f"done_{e}{tag}") for e in "TVAG"}

    def wait(self, e, after):
        for t in after:
            if t is None:
                continue
            if isinstance(t, list):
                self.wait(e, t)
                continue
            s, v = t
            if self.known[e].get(s, 0) < v:
                self.known[e][s] = v
                self.q[e].append(("wait", s, v))

    def op(self, e, fn, args, after, kw=None, inc=True):
        self.wait(e, after)
        s = self.own[e] if inc else None
        self.q[e].append(("op", fn, args, kw or {}, s, 1))
        if inc:
            self.count[s] += 1
            return (s, self.count[s])
        return None

    def dma(self, e, s, out, in_, after=()):
        self.wait(e, after)
        eng = {"S": self.nc.sync, "A": self.nc.scalar, "G": self.nc.gpsimd}[e]
        self.q[e].append(("op", eng.dma_start, (out, in_), {}, s, 16))
        self.count[s] += 16
        return (s, self.count[s])

    def wait_all(self, t):
        for e in "TVAGS":
            self.wait(e, [t])

    def branch(self, flag, tag):
        self.saved = (self.q, {e: dict(k) for e, k in self.known.items()}, self.own, flag)
        self.q = {e: [] for e in "TVAGS"}
        self.fresh(tag)

    def join(self):
        for e in "TVAGS":
            self.wait(e, [(s, self.count[s]) for s in self.own.values()])
        body = self.q
        self.q, self.known, self.own, flag = self.saved
        for e in "TVAGS":
            self.q[e].append(("if", flag, body[e]))

    def run(self, e, items):
        for it in items:
            if it[0] == "wait":
                self.eng[e].wait_ge(it[1], it[2])
            elif it[0] == "op":
                i = it[1](*it[2], **it[3])
                if it[4] is not None:
                    i.then_inc(it[4], it[5])
            else:
                r = self.eng[e].value_load(it[1])
                with self.eng[e].If(r == 1):
                    self.run(e, it[2])

    def flush(self):
        nc = self.nc
        self.eng = {"T": nc.tensor, "V": nc.vector, "A": nc.scalar, "G": nc.gpsimd, "S": nc.sync}
        block = self.ctx.enter_context(nc.Block())

        @block.tensor
        def _(e):
            self.run("T", self.q["T"])

        @block.vector
        def _(e):
            self.run("V", self.q["V"])

        @block.scalar
        def _(e):
            self.run("A", self.q["A"])

        @block.gpsimd
        def _(e):
            self.run("G", self.q["G"])

        @block.sync
        def _(e):
            self.run("S", self.q["S"])


def build(nc, d, out):
    with ExitStack() as ctx:
        pr = Prog(nc, ctx)
        program(nc, ctx, pr, d, out)
        pr.flush()


def program(nc, ctx, pr, d, out):
    def sb(name, shape, dt=F):
        return ctx.enter_context(nc.sbuf_tensor(name, shape, dt))

    V, A, G, T = nc.vector, nc.scalar, nc.gpsimd, nc.tensor

    def v(fn, args, *after, **kw):
        return pr.op("V", fn, args, after, kw)

    def a(fn, args, *after, **kw):
        return pr.op("A", fn, args, after, kw)

    def g(fn, args, *after, **kw):
        return pr.op("G", fn, args, after, kw)

    def mm(o, lhsT, rhs, start, stop, *after, inc=False, **kw):
        kw = dict(kw, start=start, stop=stop)
        return pr.op("T", T.matmul, (o, lhsT, rhs), after, kw, inc=inc)

    def act(o, i, func, *after, **kw):
        return pr.op("A", A.activation, (o, i, func), after, kw)

    def tt(o, x, y, op, *after):
        return v(V.tensor_tensor, (o, x, y, op), *after)

    def ts(o, x, s1, s2, op0, op1, *after):
        if op1 is None:
            return v(V.tensor_scalar, (o, x, s1, None, op0), *after)
        return v(V.tensor_scalar, (o, x, s1, s2, op0, op1), *after)

    def stt(o, x, s, y, op0, op1, *after):
        return v(V.scalar_tensor_tensor, (o, x, s, y, op0, op1), *after)

    def vcopy(o, i, *after):
        return v(V.tensor_copy, (o, i), *after)

    def acopy(o, i, *after):
        return act(o, i, ACT.Copy, *after)

    MUL, ADD, SUB, MAX, MIN = ALU.mult, ALU.add, ALU.subtract, ALU.max, ALU.min

    coff, cn = offsets(CONSTS)
    soff, sn = offsets(SMALLS)
    CT = sb("consts", [P, cn])
    SM = sb("smalls", [P, sn])
    X = sb("X", [P, 2, 1024])
    XT = sb("XT", [P, 8, 256])
    LG = sb("LG", [P, 2, 1024])
    RING = sb("ring", [P, NS, 4096])
    Tz = sb("Tz", [P, 4, 256])
    CS = sb("CS", [P, 2, 256])
    SC = sb("SC", [P, 1024])
    AR = sb("arena", [P, 18432 + 1024])
    PSM = ctx.enter_context(nc.psum_tensor("psum", [P, 8, 512], F))

    def C(name):
        o, n = coff[name]
        return CT[:, o:o + n]

    def S(name):
        o, n = soff[name]
        return SM[:, o:o + n]

    ident, ones = C("ident"), C("ones")[:, 0:128]

    class Area:
        at = 0

    def take(*shape):
        n = int(np.prod(shape))
        o = Area.at
        Area.at += n
        assert Area.at <= 18432 + 1024, Area.at
        w = AR[:, o:o + n]
        if len(shape) == 2:
            return w.rearrange("p (a b) -> p a b", a=shape[0])
        if len(shape) == 3:
            return w.rearrange("p (a b c) -> p a b c", a=shape[0], b=shape[1])
        return w

    free = [[] for _ in range(8)]
    turn = [0]

    def pair(fixed=None):
        i = turn[0] % 4 if fixed is None else fixed
        if fixed is None:
            turn[0] += 1
        return i, PSM[:, 2 * i:2 * i + 2, :].rearrange("p a b -> p (a b)"), free[2 * i] + free[2 * i + 1]

    def freed(i, *tokens):
        free[2 * i] = list(tokens)
        free[2 * i + 1] = list(tokens)

    ring = {"sem": [pr.sem(f"w{i}") for i in range(NS)], "n": 0, "free": [[] for _ in range(NS)]}

    def load(src, shape):
        s = ring["n"] % NS
        ring["n"] += 1
        n = int(np.prod(shape))
        dst = RING[:, s, 0:n].rearrange("p (a b) -> p a b", a=shape[0])
        t = pr.dma("S", ring["sem"][s], dst, src, ring["free"][s])
        return s, dst, t

    def release(s, *tokens):
        ring["free"][s] = list(tokens)

    def cols(w, c0, n):
        return w[:, c0:c0 + n].rearrange("(k p) n -> p k n", p=P)

    def rows(w, r0, n):
        return w[r0 * P:(r0 + n) * P, :].rearrange("(k p) n -> p k n", p=P)

    s_c, s_x, s_ln, s_o = pr.sem("c"), pr.sem("x"), pr.sem("ln"), pr.sem("o")
    pr.dma("A", s_c, CT[:, :], d["consts"])
    tC = pr.dma("A", s_c, SM[:, :], d["smalls"])
    pr.dma("A", s_x, XT[:, :, :], d["xT"].rearrange("(k p) n -> p k n", p=P))
    tX = pr.dma("A", s_x, X[:, :, :], d["x"].rearrange("(t p) n -> p t n", p=P))
    POS = sb("pos", [P, 256], I32)
    s_p = pr.sem("p")
    tP = pr.dma("A", s_p, POS[:, :], d["positions"].partition_broadcast(P))
    BV = sb("bv", [P, 512])
    tBV = pr.dma("A", s_p, BV[:, :], d["b_v"].partition_broadcast(P))
    tP = tBV

    def load_ln(gn, bn, after):
        pr.dma("A", s_ln, LG[:, 0, :], d[gn].partition_broadcast(P), after)
        return pr.dma("A", s_ln, LG[:, 1, :], d[bn].partition_broadcast(P), after)

    def rsqrt(dst, val, w, *after):
        x1, hv = w
        t = ts(x1.bitcast(I32), val.bitcast(I32), 1, None, ALU.logical_shift_right, None, *after)
        t = ts(dst.bitcast(I32), x1.bitcast(I32), -1.0, float(0x5F3759DF), MUL, ADD, t)
        t2 = ts(hv, val, -0.5, None, MUL, None, *after)
        for _ in range(3):
            t = tt(x1, dst, dst, MUL, t)
            t = tt(x1, x1, hv, MUL, t, t2)
            t = stt(dst, x1, 1.5, dst, ADD, MUL, t)
        return t

    def log1p_neg_exp(dst, x, w, *after):
        e, s, q = w
        t = ts(s, x, -1.0, None, MUL, None, *after)
        t = tt(s, x, s, MIN, t)
        t = act(e, s, ACT.Exp, t)
        t = ts(s, e, 2.0, None, ADD, None, t)
        t = v(V.reciprocal, (s, s), t)
        t = tt(s, s, e, MUL, t)
        t1 = tt(q, s, s, MUL, t)
        t = ts(dst, q, 2.0 / 19, 2.0 / 17, MUL, ADD, t1)
        for n in (15, 13, 11, 9, 7, 5, 3, 1):
            t = tt(dst, dst, q, MUL, t)
            t = ts(dst, dst, 2.0 / n, None, ADD, None, t)
        return tt(dst, dst, s, MUL, t)

    def row_scales(groups, inv_n, eps, heads, *after):
        w = len(groups) * heads
        i, ps, fr = pair()
        last = None
        for t in range(2):
            for n, chunks in enumerate(groups):
                for c, sq in enumerate(chunks):
                    o = ps[:, t * w + n * heads:t * w + (n + 1) * heads]
                    last = mm(o, sq[:, t * P:(t + 1) * P], C("bd2") if heads == 2 else ones[:, 0:1], c == 0,
                              c == len(chunks) - 1, fr, *after, inc=(t == 1 and n == len(groups) - 1 and c == len(chunks) - 1))
        val, r, w1, w2 = (SC[:, o:o + 2 * w] for o in (256, 256 + 2 * w, 256 + 4 * w, 256 + 6 * w))
        tk = None
        if isinstance(inv_n, list):
            pv = ps[:, 0:2 * w].rearrange("p (t n) -> p t n", t=2)
            vv = val.rearrange("p (t n) -> p t n", t=2)
            for n, (x, y) in enumerate(zip(inv_n, eps)):
                tk = ts(vv[:, :, n], pv[:, :, n], x, y, MUL, ADD, last)
        else:
            tk = ts(val, ps[:, 0:2 * w], inv_n, eps, MUL, ADD, last)
        freed(i, tk)
        tk = rsqrt(r, val, (w1, w2), tk)
        return r.rearrange("p (t n) -> p t n", t=2), tk

    def spread(ps, r, n, heads, *after, inc=True):
        tk = None
        for t in range(2):
            m = P // heads
            for h in range(heads):
                c = heads * n + h
                tk = mm(ps[h * m:(h + 1) * m, t * P:(t + 1) * P], r[:, t, c:c + 1].to_broadcast([P, m]), ident,
                        True, True, *after, inc=inc and t == 1 and h == heads - 1)
        return tk

    def gemm_a(ps, src, w, c0, xT, kn, *after, inc=True):
        tk = None
        for k in range(kn):
            tk = mm(ps, w[:, k, c0:c0 + src], xT[:, k, :], k == 0, k == kn - 1, *after, inc=inc and k == kn - 1)
        return tk

    def gemm_b(ps, w, c0, n, xT, t, kn, *after, inc=True):
        tk = None
        for k in range(kn):
            tk = mm(ps, xT[:, k, t * P:(t + 1) * P], w[:, k, c0:c0 + n], k == 0, k == kn - 1, *after,
                    inc=inc and k == kn - 1)
        return tk

    def four_a(w, c0, xT, kn, *after):
        i, ps, fr = pair()
        tk = None
        for c in range(4):
            tk = gemm_a(ps[:, c * 256:(c + 1) * 256], P, w, c0 + c * P, xT, kn, fr, *after, inc=c == 3)
        return i, ps, tk

    def to_xT(Z, tz, scale, bias, *after):
        outs = []
        for b in range(2):
            i, ps, fr = pair()
            tk = None
            for t in range(2):
                for k in range(4):
                    kk = 4 * b + k
                    tk = pr.op("T", T.transpose, (ps[:, k * 256 + t * P:k * 256 + (t + 1) * P],
                                                  Z[:, t, kk * P:(kk + 1) * P], ident), (fr, tz[t]), {},
                               inc=(t == 1 and k == 3))
            tks = []
            for k in range(4):
                kk = 4 * b + k
                o, s = XT[:, kk, :], ps[:, k * 256:(k + 1) * 256]
                sc = scale[:, kk:kk + 1]
                if k < 2:
                    bb = {} if bias is None else {"bias": bias[:, kk:kk + 1]}
                    x = act(o, s, ACT.Identity if bias is not None else ACT.Copy, tk, *after, scale=sc, **bb)
                elif bias is None:
                    x = ts(o, s, sc, None, MUL, None, tk, *after)
                else:
                    x = ts(o, s, sc, bias[:, kk:kk + 1], MUL, ADD, tk, *after)
                tks.append(x)
            freed(i, *tks)
            outs += tks
        return outs

    def layer_norm(banks, tb, gb, gT, bT, base, free_src):
        st = SC[:, 0:24].rearrange("p (t h s) -> p t h s", t=2, h=2)
        mv = SC[:, 24:28].rearrange("p (t s) -> p t s", t=2)
        rs, w1, w2, nb, va = (SC[:, o:o + 2] for o in (28, 30, 32, 34, 36))
        Z = take(2, 1024)
        tags, bt = [], []
        for t in range(2):
            for h in range(2):
                z = Z[:, t, h * 512:(h + 1) * 512]
                if banks is not None:
                    x = stt(z, X[:, t, h * 512:(h + 1) * 512], ALPHA, banks(t, h), MUL, ADD, tb(t, h))
                    tags.append(x)
                else:
                    z = base[:, t, h * 512:(h + 1) * 512]
                    x = tb(t, h)
                bt.append(v(V.bn_stats, (st[:, t, h, :], z), x))
        if banks is not None:
            free_src(tags)
        else:
            Z = base
        for t in range(2):
            x = v(V.bn_aggr, (mv[:, t, :], st[:, t, :, :]), *bt)
            x = ts(va[:, t:t + 1], mv[:, t, 1:2], 1e-5, None, ADD, None, x)
        x = rsqrt(rs, va, (w1, w2), x)
        x0 = v(V.scalar_tensor_tensor, (nb[:, 1:2], mv[:, 1, 0:1], -1.0, rs[:, 1:2], MUL, MUL), x)
        z1 = act(Z[:, 1, :], Z[:, 1, :], ACT.Identity, x0, scale=rs[:, 1:2], bias=nb[:, 1:2])
        z0 = ts(Z[:, 0, :], Z[:, 0, :], mv[:, 0, 0:1], rs[:, 0:1], SUB, MUL, x)
        tXT = to_xT(Z, [z0, z1], gT, bT)
        y = []
        for t, z in ((0, z0), (1, z1)):
            u = g(G.tensor_tensor, (X[:, t, :], Z[:, t, :], LG[:, 0, :], MUL), z, gb)
            y.append(g(G.tensor_tensor, (X[:, t, :], X[:, t, :], LG[:, 1, :], ADD), u))
        return y, tXT

    def rms_in(tx, gT, *after):
        Z = take(2, 1024)
        ss, va, rs, w1, w2 = (SC[:, o:o + 2] for o in (40, 42, 44, 46, 48))
        tk = []
        for t in range(2):
            tk.append(act(Z[:, t, :], X[:, t, :], ACT.Square, tx, *after, accum_out=ss[:, t:t + 1]))
        x = ts(va, ss, 1.0 / 1024, 1e-6, MUL, ADD, *tk)
        x = rsqrt(rs, va, (w1, w2), x)
        z0 = ts(Z[:, 0, :], X[:, 0, :], rs[:, 0:1], None, MUL, None, x)
        z1 = act(Z[:, 1, :], X[:, 1, :], ACT.Copy, x, scale=rs[:, 1:2])
        return to_xT(Z, [z0, z1], gT, None)

    def bias_table():
        i, ps, fr = pair()
        R4, TB = take(384), take(4, 256)
        tk = mm(ps[0:4, 0:384], S("relb")[0:32, :], C("oh")[0:32, :], True, True, tC, inc=True)
        x = vcopy(R4[0:4, :], ps[0:4, 0:384], tk)
        freed(i, x)
        s_t = pr.sem("tz")
        y = pr.dma("S", s_t, d["scratch"], R4[0:4, :], [x])
        base = d["scratch"]
        y = pr.dma("S", s_t, TB, bass.AP(tensor=base.tensor, offset=base.offset, ap=[[1, P], [384, 4], [1, 256]]), [y])
        i, ps, fr = pair()
        for n in range(2):
            tk = mm(ps[:, n * 512:(n + 1) * 512], C("anti"), TB[:, 2 * n:2 * n + 2, :].rearrange("p a b -> p (a b)"),
                    True, True, fr, y, inc=n == 1)
        x = tt(Tz[:, :, :], ps.rearrange("p (h j) -> p h j", h=4), C("maskM").unsqueeze(1).to_broadcast([P, 4, 256]),
               ADD, tk)
        freed(i, x)
        return x

    def trig():
        pf, an, kk, rr = (take(256) for _ in range(4))
        x = vcopy(pf, POS[:, :], tP)
        x = ts(an, pf, C("invf"), None, MUL, None, x, tC)
        for n in range(2):
            y = ts(kk, an, 1.0 / (2 * math.pi), 0.25 if n == 0 else 0.0, MUL, ADD, x)
            y = ts(kk, kk, 12582912.0, -12582912.0, ADD, ADD, y)
            y = stt(rr, kk, -6.28125, an, MUL, ADD, y)
            y = stt(rr, kk, -0.0019340515136718750, rr, MUL, ADD, y)
            y = stt(rr, kk, -(2 * math.pi - 6.28125 - 0.0019340515136718750), rr, MUL, ADD, y)
            if n == 0:
                y = ts(rr, rr, math.pi / 2, None, ADD, None, y)
            y = ts(rr, rr, 3.1415925, -3.1415925, MIN, MAX, y)
            x = act(CS[:, n, :], rr, ACT.Sin, y)
        return x

    def soft(u, L, bias_ap, scale, tlog, psidx, ps, W, sink=None):
        base = 64 + 16 * (u % 8)
        nm, sm = SC[:, base:base + 4], SC[:, base + 4:base + 8]
        if sink is None:
            x = stt(L, ps, scale, bias_ap, MUL, ADD, tlog)
        else:
            for b in range(2):
                x = stt(L[:, 2 * b:2 * b + 2, :], ps[:, b], scale, bias_ap, MUL, ADD, tlog)
        freed(psidx, x)
        x = v(V.tensor_reduce, (nm, L, AX, MAX), x, negate=True)
        if sink is not None:
            x = tt(nm, nm, sink[0], MIN, x)
            sk = SC[:, base + 8:base + 12]
            y = tt(sk, nm, sink[1], ADD, x)
        tk = []
        for h in range(4):
            tk.append(act(L[:, h, :], L[:, h, :], ACT.Exp, x, bias=nm[:, h:h + 1], accum_out=sm[:, h:h + 1]))
        if sink is not None:
            z = act(sk, sk, ACT.Exp, y)
            z = tt(sm, sm, sk, ADD, z, *tk)
            tk.append(z)
        r = SC[:, base + 12:base + 16]
        z = v(V.reciprocal, (r, sm), *tk)
        return r, z

    def diags(D, r, factor, *after):
        tk = None
        for h in range(4):
            if factor is None:
                tk = ts(D[:, h, :], ident, r[:, h:h + 1], None, MUL, None, *after)
            else:
                tk = ts(D[:, h, :], ident, r[:, h:h + 1], factor, MUL, MUL, *after)
        return tk

    def pT(u, parts, t, PT, W, *after):
        i, ps, fr = pair()
        tk = None
        nb = W // P
        for h in range(4):
            for kb in range(nb):
                o = ps[:, (h * nb + kb) * P:(h * nb + kb + 1) * P]
                for n, (L, D, tl) in enumerate(parts):
                    tk = mm(o, L[:, h, kb * P:(kb + 1) * P], D[:, h, :], n == 0, n == len(parts) - 1, fr, tl,
                            inc=(h == 3 and kb == nb - 1 and n == len(parts) - 1))
        src = ps[:, 0:4 * W].rearrange("p (h x) -> p h x", h=4)
        if W == P:
            x = [vcopy(PT[:, :, 0:W], src, tk, *after)]
        else:
            x = [vcopy(PT[:, 0:2, 0:W], src[:, 0:2, :], tk, *after), acopy(PT[:, 2:4, 0:W], src[:, 2:4, :], tk, *after)]
        freed(i, *x)
        return x

    state = {}

    def mixer1(l, tXT):
        Area.at = 0
        lam0 = 0.8 - 0.6 * math.exp(-0.3 * l)
        w = d[f"w_in{l}"]
        QT, QR, KT, DQ, DK = take(4, 256), take(4, 256), take(4, 256), take(4, 256), take(4, 256)
        KR = take(256)
        VM, DV = take(2, 512), take(2, 512)
        CC, SQ = take(5, 256), take(5, 256)
        MT = take(8, 256)
        Ls = [take(4, 256) for _ in range(3)]
        Ds = [take(4, 128) for _ in range(2)]
        PTs = [take(4, 256)]
        lam = SC[:, 200:212]
        dl = S(f"dl{l}")
        x = tt(lam[0:64, 0:1], dl[0:64, 0:1], dl[0:64, 1:2], MUL, tC)
        x = tt(lam[0:64, 1:2], dl[0:64, 2:3], dl[0:64, 3:4], MUL, x)
        s0, w0, t0 = load(cols(w, 0, 512), (8, 512))
        i0, p0, k0 = four_a(w0, 0, XT, 8, t0, tXT)
        release(s0, k0)
        s1, w1, t1 = load(cols(w, 512, 512), (8, 512))
        i1, p1, k1 = four_a(w1, 0, XT, 8, t1)
        release(s1, k1)
        iL, pL, fL = pair()
        kL = mm(pL[:, 0:2], C("ones")[0:64, 0:128], lam[0:64, 0:2], True, True, fL, x, inc=True)
        x = act(lam[:, 2:4], pL[:, 0:2], ACT.Exp, kL)
        freed(iL, x)
        x = tt(lam[:, 4:5], lam[:, 3:4], lam[:, 2:3], SUB, x)
        tlam = ts(lam[:, 4:5], lam[:, 4:5], -lam0, None, ADD, None, x)
        nlam = lam[:, 4:5]
        c0 = vcopy(CC[:, 0:4, :].rearrange("p a b -> p (a b)"), p0, k0)
        q0 = act(SQ[:, 0:4, :], CC[:, 0:4, :], ACT.Square, c0)
        freed(i0, c0)
        c1 = vcopy(CC[:, 4, :], p1[:, 0:256], k1)
        q1 = act(SQ[:, 4, :], CC[:, 4, :], ACT.Square, c1)
        KC = Ls[0][:, 0, :]
        ckr = tt(KC, p1[:, 256:512], C("cos1"), MUL, k1)
        cdq = acopy(DQ[:, 0:2, :].rearrange("p a b -> p (a b)"), p1[:, 512:1024], k1)
        freed(i1, c1, ckr, cdq)
        s2, w2, t2 = load(cols(w, 1024, 512), (8, 512))
        i2, p2, k2 = four_a(w2, 0, XT, 8, t2)
        release(s2, k2)
        r, tr = row_scales([[SQ[:, c, :] for c in range(3)], [SQ[:, c, :] for c in (3, 4)]],
                           [1.0 / 384, 1.0 / 256], [1e-6, 1e-6], 1, q0, q1)
        x2 = acopy(DQ[:, 2:4, :].rearrange("p a b -> p (a b)"), p2[:, 0:512], k2)
        y2 = vcopy(DK[:, 0:2, :].rearrange("p a b -> p (a b)"), p2[:, 512:1024], k2)
        freed(i2, x2, y2)
        s3, w3, t3 = load(cols(w, 1792, 512), (8, 512))
        i3, p3, f3 = pair()
        for t in range(2):
            k3 = gemm_b(p3[:, t * 512:(t + 1) * 512], w3, 0, 512, XT, t, 8, f3, t3, inc=t == 1)
        release(s3, k3)
        cdv = acopy(DV.rearrange("p a b -> p (a b)"), p3, k3)
        freed(i3, cdv)
        i4, p4, f4 = pair()
        spread(p4[:, 0:256], r, 0, 1, f4, tr, inc=False)
        k4 = spread(p4[:, 256:512], r, 1, 1, tr)
        kf = mm(p4[:, 512:768], C("fold"), KC, True, True, ckr, inc=True)
        tn = []
        for c in range(5):
            sc = S(f"qn{l}")[:, c:c + 1] if c < 3 else S(f"kvn{l}")[:, c - 3:c - 2]
            rb = p4[:, 0:256] if c < 3 else p4[:, 256:512]
            tn.append(stt(CC[:, c, :], CC[:, c, :], sc, rb, MUL, MUL, k4, c0, c1, q0, q1))
        ckr = vcopy(KR, p4[:, 512:768], kf)
        freed(i4, tn[-1], ckr)
        s4, w4, t4 = load(cols(w, 1536, 256), (8, 256))
        i5, p5, f5 = pair()
        gemm_a(p5[:, 0:256], P, w4, 0, XT, 8, f5, t4, inc=False)
        k5 = gemm_a(p5[:, 256:512], P, w4, 128, XT, 8)
        release(s4, k5)
        x5 = acopy(DK[:, 2:4, :].rearrange("p a b -> p (a b)"), p5[:, 0:512], k5)
        freed(i5, x5)
        s5, w5, t5 = load(cols(d[f"w_uq{l}"], 0, 1024), (3, 1024))
        i6, p6, k6 = four_a(w5, 0, CC, 3, t5, tn)
        i7, p7, k7 = four_a(w5, 512, CC, 3)
        release(s5, k7)
        cq = acopy(QT.rearrange("p a b -> p (a b)"), p6, k6)
        freed(i6, cq)
        cr = tt(QR, p7.rearrange("p (a b) -> p a b", a=4), C("cos1").unsqueeze(1).to_broadcast([P, 4, 256]), MUL, k7)
        freed(i7, cr)
        s6, w6, t6 = load(cols(d[f"w_ukv{l}"], 0, 1024), (2, 1024))
        i8, p8, k8 = four_a(w6, 0, CC[:, 3:5, :], 2, t6)
        ck = acopy(KT.rearrange("p a b -> p (a b)"), p8, k8)
        freed(i8, ck)
        i9, p9, f9 = pair()
        for t in range(2):
            k9 = gemm_b(p9[:, t * 512:(t + 1) * 512], w6, 512, 512, CC[:, 3:5, :], t, 2, f9, inc=t == 1)
        release(s6, k9)
        cv = vcopy(VM.rearrange("p a b -> p (a b)"), p9, k9)
        freed(i9, cv)

        def logits_mla(u, t, L, D):
            W = P * (t + 1)
            i, ps, fr = pair()
            tk = None
            for h in range(4):
                o = ps[:, h * W:(h + 1) * W]
                mm(o, QT[:, h, t * P:(t + 1) * P], KT[:, h, 0:W], True, False, fr, cq, ck)
                tk = mm(o, QR[:, h, t * P:(t + 1) * P], KR[:, 0:W], False, True, cr, ckr, inc=h == 3)
            m = C("maskM")[:, 256 - W:256].unsqueeze(1).to_broadcast([P, 4, W])
            r, z = soft(u, L[:, :, 0:W], m, (192) ** -0.5, tk, i, ps[:, 0:4 * W].rearrange("p (h x) -> p h x", h=4), W)
            return [(L, D, diags(D, r, None, z))], W, t, 0

        def logits_diff(u, t, L2, D2):
            W = P * (t + 1)
            parts = []
            for c in range(2):
                L, D = L2[c], D2[c]
                i, ps, fr = pair()
                tk = None
                for h in range(4):
                    o = ps[:, h * W:(h + 1) * W]
                    tk = mm(o, DQ[64 * c:64 * c + 64, h, t * P:(t + 1) * P], DK[64 * c:64 * c + 64, h, 0:W], True, True,
                            fr, cdq, x2, y2, x5, inc=h == 3)
                r, z = soft(u + c, L[:, :, 0:W], Tz[:, :, 256 - W:256], 0.125, tk, i,
                            ps[:, 0:4 * W].rearrange("p (h x) -> p h x", h=4), W)
                parts.append((L, D, diags(D, r, None if c == 0 else nlam, z, tlam)))
            return parts, W, t, 4

        mt = {}

        def finish(u):
            parts, W, t, base = u
            PT = PTs[0]
            x = pT(0, parts, t, PT, W, state.get("pt"))
            i, ps, fr = pair()
            tk = None
            VV = VM if base == 0 else DV
            for h in range(4):
                for kb in range(W // P):
                    tk = mm(ps[:, h * P:(h + 1) * P], VV[:, kb, h * P:(h + 1) * P], PT[:, h, kb * P:(kb + 1) * P],
                            kb == 0, kb == W // P - 1, fr, x, cv, cdv, inc=(h == 3 and kb == W // P - 1))
            state["pt"] = tk
            z = acopy(MT[:, base:base + 4, t * P:(t + 1) * P], ps[:, 0:512].rearrange("p (h x) -> p h x", h=4), tk)
            freed(i, z)
            mt[(base, t)] = z

        u0 = logits_mla(0, 0, Ls[0], Ds[0])
        u1 = logits_mla(1, 1, Ls[1], Ds[1])
        finish(u0)
        finish(u1)
        u2 = logits_diff(2, 0, (Ls[2], Ls[0]), (Ds[0], Ds[1]))
        finish(u2)
        u3 = logits_diff(4, 1, (Ls[1], Ls[2]), (Ds[0], Ds[1]))
        finish(u3)
        sq = act(SQ[:, 0:4, :], MT[:, 4:8, :], ACT.Square, mt[(4, 0)], mt[(4, 1)])
        r, tr = row_scales([[SQ[:, h, :]] for h in range(4)], 1.0 / 128, 1e-5, 1, sq)
        i, ps, fr = pair()
        for h in range(4):
            tk = spread(ps[:, h * 256:(h + 1) * 256], r, h, 1, fr, tr, inc=h == 3)
        dn = SC[:, 220:221]
        x = ts(dn, S(f"dn{l}"), 1.0 - lam0, None, MUL, None)
        x = stt(MT[:, 4:8, :], MT[:, 4:8, :], dn, ps.rearrange("p (h x) -> p h x", h=4), MUL, MUL, tk, x, sq)
        freed(i, x)
        return MT, [x, mt[(0, 0)], mt[(0, 1)]]

    def project(MT, w, *after):
        res = {}
        idx = []
        for h in range(2):
            s, ww, t0 = load(cols(w, h * 512, 512), (8, 512))
            i, ps, fr = pair()
            idx.append(i)
            for t in range(2):
                res[(t, h)] = (ps[:, t * 512:(t + 1) * 512],
                               gemm_b(ps[:, t * 512:(t + 1) * 512], ww, 0, 512, MT, t, 8, fr, t0, *after))
            release(s, res[(1, h)][1])
        return res, idx

    def ffn(wg, wu, wd, nf, hidden):
        y = [PSM[:, b, :] for b in range(4)]
        yf = [list(free[b]) for b in range(4)]
        pend = []
        n = [0]
        last = [None]

        def down(j, hT, th, wdv, rel):
            for t in range(2):
                for h in range(2):
                    b = t * 2 + h
                    last[0] = mm(y[b], hT[:, t * P:(t + 1) * P], wdv[:, h * 512:(h + 1) * 512], j == 0, j == nf - 1,
                                 th, yf[b], inc=(t == 1 and h == 1))
            return last[0]

        jj = 0
        for gi in range((nf + 3) // 4):
            m = min(4, nf - 4 * gi)
            sg, vg, tg = load(cols(wg, gi * 512, m * P), (8, m * P))
            su, vu, tu = load(cols(wu, gi * 512, m * P), (8, m * P))
            sd, vd, td = load(rows(wd, gi * 4, m), (m, 1024))
            for c in range(m):
                b = 4 + jj % 4
                ps = PSM[:, b, :]
                gemm_a(ps[:, 0:256], P, vg, c * P, XT, 8, tg, free[b], state["xt"], inc=False)
                tk = gemm_a(ps[:, 256:512], P, vu, c * P, XT, 8, tu)
                hT, th, fb = hidden(jj, ps, tk)
                free[b] = fb
                if c == m - 1:
                    release(sg, tk)
                    release(su, tk)
                pend.append((jj, hT, [th, td], vd[:, c, :], sd if c == m - 1 else None))
                if len(pend) > 1:
                    q = pend.pop(0)
                    tq = down(*q)
                    hfree[q[0] % 4] = tq
                    if q[4] is not None:
                        release(q[4], tq)
                jj += 1
        while pend:
            q = pend.pop(0)
            tq = down(*q)
            if q[4] is not None:
                release(q[4], tq)
        return y, tq

    hfree = [None] * 4

    def swiglu_hidden(HT, TH):
        def f(j, ps, tk):
            k = j % 4
            x = act(TH[:, k, :], ps[:, 0:256], ACT.Tanh, tk, hfree[k], scale=0.5)
            y = stt(TH[:, k, :], TH[:, k, :], 1.0, ps[:, 0:256], ADD, MUL, x)
            z = stt(HT[:, k, :], TH[:, k, :], 0.5, ps[:, 256:512], MUL, MUL, y, hfree[k])
            return HT[:, k, :], z, [z]
        return f

    def conv_hidden(l, HT, TH, CV):
        fw, fb = S(f"fcw{l}").rearrange("p (j c) -> p j c", j=3), S(f"fcb{l}")

        def f(j, ps, tk):
            k = j % 4
            c, q, gp = CV[:, k, :], TH[:, k, :], ps[:, 0:256]
            x = ts(c, gp, fw[:, 2, j:j + 1], fb[:, j:j + 1], MUL, ADD, tk, hfree[k])
            x = stt(c[:, 1:256], gp[:, 0:255], fw[:, 1, j:j + 1], c[:, 1:256], MUL, ADD, x)
            x = stt(c[:, 2:256], gp[:, 0:254], fw[:, 0, j:j + 1], c[:, 2:256], MUL, ADD, x)
            y = act(q, c, ACT.Square, x)
            y = ts(q, q, 0.044715, 1.0, MUL, ADD, y)
            y = tt(q, q, c, MUL, y)
            y = act(q, q, ACT.Tanh, y, scale=GELU_C)
            y = stt(q, q, 1.0, c, ADD, MUL, y)
            z = stt(HT[:, k, :], q, 0.5, ps[:, 256:512], MUL, MUL, y)
            return HT[:, k, :], z, [z]
        return f

    def add_alpha_free(y):
        def fr(tags):
            for b in range(4):
                free[b] = [tags[b]]
        return fr

    def moe(xr, tXT, tLG):
        Area.at = 0
        NP = 256 // CAP
        ACC = take(2, 1024)
        XE = [take(8, CAP) for _ in range(2)]
        SE = [take(2, CAP) for _ in range(2)]
        SW = [take(2, CAP) for _ in range(2)]
        GT = [take(256) for _ in range(2)]
        YE = take(1024)
        HT = [take(2 * CAP) for _ in range(4)]
        TH = [take(2 * CAP) for _ in range(4)]
        L, pos, msk, gate, rank, s2 = (SC[:, 512 + 16 * n:528 + 16 * n] for n in range(6))
        T8 = SC[:, 608:624]
        gt = SC[:, 640:768]
        eq = SC[:, 768:896]
        sm = SC[:, 896:920]
        FL = sb("flag", [P, 8], I32)
        i, ps, fr = pair(2)
        for t in range(2):
            for k in range(8):
                tk = mm(ps[:, t * 8:(t + 1) * 8], XT[:, k, t * P:(t + 1) * P], S("router")[:, k * 8:(k + 1) * 8],
                        k == 0, k == 7, fr, tXT, inc=(t == 1 and k == 7))
        x = vcopy(L, ps[:, 0:16], tk)
        freed(2, x)
        for t in range(2):
            y = v(V.max, (T8[:, t * 8:(t + 1) * 8], L[:, t * 8:(t + 1) * 8]), x)
        Lv = L.rearrange("p (t e) -> p t e", t=2)
        g4 = gt.rearrange("p (t e j) -> p t e j", t=2, e=8)
        e4 = eq.rearrange("p (t e j) -> p t e j", t=2, e=8)
        z = None
        for t in range(2):
            lj = Lv[:, t, :].unsqueeze(1).to_broadcast([P, 8, 8])
            le = Lv[:, t, :].unsqueeze(2).to_broadcast([P, 8, 8])
            tt(g4[:, t], lj, le, ALU.is_gt, x)
            z = tt(e4[:, t], lj, le, ALU.is_equal, x)
            z = tt(e4[:, t], e4[:, t], C("tri8").rearrange("p (e j) -> p e j", e=8), MUL, z)
            z = tt(g4[:, t], g4[:, t], e4[:, t], ADD, z)
        z = v(V.tensor_reduce, (rank, gt.rearrange("p (n j) -> p n j", j=8), AX, ADD), z)
        tv = T8.rearrange("p (t e) -> p t e", t=2)
        q = tt(sm[:, 0:2], tv[:, :, 1], tv[:, :, 0], SUB, y)
        q = act(sm[:, 2:4], sm[:, 0:2], ACT.Exp, q)
        q = ts(sm[:, 4:6], sm[:, 2:4], 1.0, None, ADD, None, q)
        q = v(V.reciprocal, (sm[:, 4:6], sm[:, 4:6]), q)
        q = tt(sm[:, 6:8], sm[:, 4:6], sm[:, 2:4], MUL, q)
        s1 = ts(msk, rank, 0.0, None, ALU.is_equal, None, z)
        z2 = ts(s2, rank, 1.0, None, ALU.is_equal, None, z)
        for t in range(2):
            r = slice(t * 8, (t + 1) * 8)
            z3 = ts(gate[:, r], msk[:, r], sm[:, 4 + t:5 + t], None, MUL, None, s1, q)
            z3 = stt(gate[:, r], s2[:, r], sm[:, 6 + t:7 + t], gate[:, r], MUL, ADD, z3, z2)
        tm = tt(msk, msk, s2, ADD, z3)
        i, ps, fr = pair(2)
        mm(ps[:, 0:8], C("tri"), msk[:, 0:8], True, True, fr, tm)
        mm(ps[:, 8:16], C("tri"), msk[:, 8:16], True, False)
        mm(ps[:, 8:16], ones, msk[:, 0:8], False, True)
        mm(ps[:, 16:24], ones, msk[:, 0:8], True, False)
        tk = mm(ps[:, 16:24], ones, msk[:, 8:16], False, True, inc=True)
        tpos = vcopy(pos, ps[:, 0:16], tk)
        x = v(V.tensor_reduce, (sm[:, 8:9], ps[:, 16:24], AX, MAX), tk)
        freed(2, tpos, x)
        tfl = None
        for p in range(1, NP):
            y = ts(sm[:, 8 + p:9 + p], sm[:, 8:9], float(p * CAP), None, ALU.is_gt, None, x)
            tfl = vcopy(FL[:, p:p + 1], sm[:, 8 + p:9 + p], y)
        tacc = {0: act(ACC[:, 0, :], X[:, 0, :], ACT.Copy, xr, scale=ALPHA),
                1: act(ACC[:, 1, :], X[:, 1, :], ACT.Copy, xr, scale=ALPHA)}

        def one_pass(p):
            st = {"xe": [None, None], "gt": [None, None], "h": [None] * 4, "y": None}

            def prepare(e):
                b = e % 2
                o = p * CAP
                for t in range(2):
                    n = t * 8 + e
                    io = C("iota")[:, o:o + CAP]
                    x = ts(SE[b][:, t, :], io, pos[:, n:n + 1], msk[:, n:n + 1], ALU.is_equal, MUL, tpos, st["xe"][b])
                    y = ts(SW[b][:, t, :], io, pos[:, n:n + 1], gate[:, n:n + 1], ALU.is_equal, MUL, st["gt"][b])
                i, ps, fr = pair(2)
                for t in range(2):
                    tk = pr.op("T", T.transpose, (ps[0:CAP, t * P:(t + 1) * P], SW[b][:, t, :], ident), (fr, y), {},
                               inc=t == 1)
                z = acopy(GT[b][0:CAP, :], ps[0:CAP, 0:256], tk, st["gt"][b])
                freed(2, z)
                tgt[b] = z
                i, ps, fr = pair(2)
                for k in range(8):
                    for t in range(2):
                        tk = mm(ps[:, k * CAP:(k + 1) * CAP], X[:, t, k * P:(k + 1) * P], SE[b][:, t, :], t == 0, t == 1,
                                fr, x, xr, inc=(k == 7 and t == 1))
                src = ps[:, 0:8 * CAP].rearrange("p (k c) -> p k c", k=8)
                q1 = acopy(XE[b][:, 0:4, :], src[:, 0:4, :], tk, st["xe"][b])
                q2 = vcopy(XE[b][:, 4:8, :], src[:, 4:8, :], tk, st["xe"][b], q1 if CAP < 128 else None)
                freed(2, q1, q2)
                txe[b] = [q1, q2]

            txe, tgt = {}, {}

            def scatter(e):
                b = e % 2
                for t in range(2):
                    i, ps, fr = pair(3)
                    for h in range(2):
                        tk = mm(ps[:, h * 512:(h + 1) * 512], GT[b][0:CAP, t * P:(t + 1) * P],
                                YE[0:CAP, h * 512:(h + 1) * 512], True, True, fr, tgt[b], st["ye"], inc=h == 1)
                    x = tt(ACC[:, t, :], ACC[:, t, :], ps, ADD, tk, tacc[t])
                    tacc[t] = x
                    freed(3, x)
                st["gt"][b] = tk
                st["yread"] = tk

            st["yread"] = None
            prepare(0)
            n = 0
            for e in range(8):
                b = e % 2
                pend = []
                yf = list(free[2]) + list(free[3])

                def down(hT, th, vd, cc, sd, first, last):
                    tk = None
                    for c in range(2):
                        for h in range(2):
                            tk = mm(PSM[0:CAP, 2 + h, :], hT[:, c * CAP:(c + 1) * CAP], vd[:, cc + c, h * 512:(h + 1) * 512],
                                    first and c == 0, last and c == 1, th, yf, inc=(c == 1 and h == 1))
                    return tk

                for gi in range(7):
                    sg, vg, tg = load(cols(d["moe_g"][e], gi * 512, 512), (8, 512))
                    su, vu, tu = load(cols(d["moe_u"][e], gi * 512, 512), (8, 512))
                    sd, vd, td = load(rows(d["moe_d"][e], gi * 4, 4), (4, 1024))
                    for c2 in range(2):
                        k = n % 4
                        bk = n % 2
                        ps = PSM[:, bk, :]
                        xe = XE[b]
                        for c in range(2):
                            cc = (2 * c2 + c) * P
                            gemm_a(ps[:, c * CAP:(c + 1) * CAP], P, vg, cc, xe, 8, tg, free[bk], txe[b], inc=False)
                            tk = gemm_a(ps[:, (2 + c) * CAP:(3 + c) * CAP], P, vu, cc, xe, 8, tu, inc=c == 1)
                        gp, up = ps[:, 0:2 * CAP], ps[:, 2 * CAP:4 * CAP]
                        x = act(TH[k], gp, ACT.Tanh, tk, st["h"][k], scale=0.5)
                        y = stt(TH[k], TH[k], 1.0, gp, ADD, MUL, x)
                        z = stt(HT[k], TH[k], 0.5, up, MUL, MUL, y, st["h"][k])
                        free[bk] = [z]
                        if c2 == 1:
                            release(sg, tk)
                            release(su, tk)
                        last = gi == 6 and c2 == 1
                        pend.append((k, HT[k], [z, td], vd, 2 * c2, sd if c2 else None, gi == 0 and c2 == 0, last))
                        while len(pend) > (0 if last else 1):
                            q = pend.pop(0)
                            tq = down(*q[1:])
                            st["h"][q[0]] = tq
                            if q[5] is not None:
                                release(q[5], tq)
                        n += 1
                    if gi == 1 and e > 0:
                        scatter(e - 1)
                    if gi == 3 and e < 7:
                        prepare(e + 1)
                st["xe"][b] = tk
                y1 = vcopy(YE[0:CAP, 0:512], PSM[0:CAP, 2, :], tq, st["yread"])
                y2 = acopy(YE[0:CAP, 512:1024], PSM[0:CAP, 3, :], tq, st["yread"])
                st["ye"] = [y1, y2]
                free[2] = [y1]
                free[3] = [y2]
            scatter(7)

        one_pass(0)
        for p in range(1, NP):
            pr.wait_all(tfl)
            saved = (ring["sem"], list(ring["free"]), [list(x) for x in free], dict(tacc), ring["n"])
            pr.branch(FL[0:1, p:p + 1], f"_{p}")
            ring["sem"] = [pr.sem(f"w{i}_{p}") for i in range(NS)]
            one_pass(p)
            pr.join()
            ring["sem"], ring["free"], fr, ta, ring["n"] = saved
            for i in range(8):
                free[i] = fr[i]
            tacc.update(ta)
        return layer_norm(None, lambda t, h: tacc[t], tLG, S("g21"), S("b21"), ACC, None)

    def conv(dst, src, w, c, b, *after):
        x = ts(dst, src, w[:, 3, c:c + 1], b, MUL, ADD, *after)
        for s in range(1, 4):
            x = stt(dst[:, s:256], src[:, 0:256 - s], w[:, 3 - s, c:c + 1], dst[:, s:256], MUL, ADD, x)
        return x

    def hybrid(tXT):
        w = d["hy_w"]
        XR, GR, QK, VV, OO = take(4, 256), take(4, 256), take(8, 256), take(2, 512), take(4, 256)
        XC, QC, MT = take(4, 256), take(8, 256), take(8, 256)
        TR, TI, AA = take(4, 256), take(4, 256), take(4, 256)
        L, D, PT = take(4, 256), take(4, 128), take(4, 256)
        ROW = take(8, 256)
        flat = "p a b -> p (a b)"
        bn = S("bin")

        def proj(dst, n0, col):
            s, ww, t0 = load(cols(w, col, 512), (8, 512))
            i, ps, tk = four_a(ww, 0, XT, 8, t0, tXT)
            release(s, tk)
            out = []
            for c in range(4):
                o, src, b = dst[:, c, :], ps[:, c * 256:(c + 1) * 256], bn[:, n0 + c:n0 + c + 1]
                if c >= 2:
                    out.append(act(o, src, ACT.Identity, tk, bias=b))
                else:
                    out.append(ts(o, src, b, None, ADD, None, tk))
            freed(i, *out)
            return out

        def conv_silu(src, dst, c0, tin):
            out = []
            mw = S("mcw").rearrange("p (j c) -> p j c", j=4)
            for c in range(4):
                x = conv(dst[:, c, :], src[:, c, :], mw, c0 + c, S("mcb")[:, c0 + c:c0 + c + 1], *tin)
                y = act(src[:, c, :], dst[:, c, :], ACT.Tanh, x, scale=0.5)
                out.append(stt(dst[:, c, :], src[:, c, :], 1.0, dst[:, c, :], ADD, MUL, y))
            return out

        wif = S("wif").rearrange("p (k n) -> p k n", k=8)
        i, ps, fr = pair()
        gemm_a(ps[0:4, 0:256], 4, wif, 0, XT, 8, fr, tXT, inc=False)
        tk = gemm_a(ps[0:4, 256:512], 4, wif, 4, XT, 8)
        R = [ROW[0:4, n, :] for n in range(8)]
        ri = ts(R[0], ps[0:4, 0:256], S("bif")[0:4, 0:1], None, ADD, None, tk)
        rf = ts(R[1], ps[0:4, 256:512], S("bif")[0:4, 1:2], None, ADD, None, tk)
        freed(i, ri, rf)
        x = log1p_neg_exp(R[5], R[1], (R[2], R[3], R[4]), rf)
        x = stt(R[5], R[1], 0.0, R[5], MIN, SUB, x)
        x = v(V.tensor_tensor_scan, (R[2], C("ones")[0:4, :], R[5], 0.0, MUL, ADD), x)
        x = tt(R[0], R[0], R[2], SUB, x, ri)
        trow = x
        x = v(V.tensor_tensor_scan, (R[3], C("ones")[0:4, :], R[0], -3.0e38, MUL, MAX), x)
        tmr = tt(R[4], R[2], R[3], ADD, x)
        nsp, w1, w2, w3 = (SC[:, 512 + 4 * n:516 + 4 * n] for n in range(4))
        x = log1p_neg_exp(nsp, S("lam"), (w1, w2, w3))
        x = ts(w1, S("lam"), -1.0, 0.0, MUL, MAX, x)
        x = tt(nsp, nsp, w1, ADD, x)
        tns = ts(nsp, nsp, -4.0, None, MUL, None, x)
        hba, hbx = SC[:, 528:532], SC[:, 532:536]
        tha = ts(hba, S("rba"), 0.5, None, MUL, None)
        thx = ts(hbx, S("rbx"), 0.5, None, MUL, None)

        tq0 = proj(QK[:, 0:4, :], 8, 1024)
        tk0 = proj(QK[:, 4:8, :], 12, 1536)
        txr = proj(XR, 0, 0)
        s, ww, t0 = load(cols(w, 2048, 512), (8, 512))
        i, ps, fr = pair()
        for t in range(2):
            tk = gemm_b(ps[:, t * 512:(t + 1) * 512], ww, 0, 512, XT, t, 8, fr, t0, inc=t == 1)
        release(s, tk)
        tv = tt(VV, ps.rearrange("p (t n) -> p t n", t=2), BV[:, :].unsqueeze(1).to_broadcast([P, 2, 512]), ADD, tk, tBV)
        freed(i, tv)
        tgr = proj(GR, 4, 512)
        too = proj(OO, 20, 2560)
        tq = conv_silu(QK[:, 0:4, :], QC[:, 0:4, :], 0, tq0)
        tkk = conv_silu(QK[:, 4:8, :], QC[:, 4:8, :], 4, tk0)
        i, ps, fr = pair()
        for t in range(2):
            pr.op("T", T.transpose, (ps[:, t * 8:t * 8 + 4], R[3][:, t * P:(t + 1) * P], ident[0:4, 0:4]), (fr, tmr), {}, inc=False)
            tk = pr.op("T", T.transpose, (ps[:, t * 8 + 4:t * 8 + 8], R[4][:, t * P:(t + 1) * P], ident[0:4, 0:4]), (), {},
                       inc=t == 1)
        GC = SC[:, 540:556]
        tgc = ts(GC, ps[:, 0:16], -1.0, None, MUL, None, tk)
        freed(i, tgc)
        EM = SC[:, 556:572]
        tem = act(EM, GC, ACT.Exp, tgc)

        def unit(t, *after):
            W = P * (t + 1)
            i, ps, fr = pair()
            for h in range(4):
                tk = mm(ps[:, h * W:(h + 1) * W], C("sel4")[0:4, h * P:(h + 1) * P], R[0][:, 0:W], True, True, fr, trow,
                        inc=h == 3)
            Lw = L[:, :, 0:W]
            x = tt(Lw, ps[:, 0:4 * W].rearrange("p (h x) -> p h x", h=4),
                   C("maskM")[:, 256 - W:256].unsqueeze(1).to_broadcast([P, 4, W]), ADD, tk, *after)
            freed(i, x)
            i, ps, fr = pair()
            for h in range(4):
                tk = mm(ps[:, h * W:(h + 1) * W], QC[:, h, t * P:(t + 1) * P], QC[:, 4 + h, 0:W], True, True, fr, tq, tkk,
                        inc=h == 3)
            ee = [act(L[:, h, 0:W], L[:, h, 0:W], ACT.Exp, x, tgc, bias=GC[:, t * 8 + h:t * 8 + h + 1]) for h in range(4)]
            x = stt(Lw, ps[:, 0:4 * W].rearrange("p (h x) -> p h x", h=4), 0.25 * 128 ** -0.5, Lw, MUL, MUL, tk, *ee)
            freed(i, x)
            o = 576 + 16 * t
            dn, nd = SC[:, o:o + 4], SC[:, o + 4:o + 8]
            x = v(V.tensor_reduce, (dn, Lw, AX, ADD), x)
            x = ts(nd, dn, -1.0, None, MUL, None, x)
            x = tt(dn, dn, nd, MAX, x)
            x = tt(dn, dn, EM[:, t * 8 + 4:t * 8 + 8], MAX, x, tem)
            x = v(V.reciprocal, (dn, dn), x)
            x = diags(D, dn, None, x)
            z = pT(0, [(L, D, x)], t, PT, W, state.get("pt2"))
            i, ps, fr = pair()
            for h in range(4):
                for kb in range(W // P):
                    tk = mm(ps[:, h * P:(h + 1) * P], VV[:, kb, h * P:(h + 1) * P], PT[:, h, kb * P:(kb + 1) * P],
                            kb == 0, kb == W // P - 1, fr, z, tv, inc=(h == 3 and kb == W // P - 1))
            state["pt2"] = tk
            y = acopy(MT[:, 4:8, t * P:(t + 1) * P], ps[:, 0:512].rearrange("p (h x) -> p h x", h=4), tk)
            freed(i, y)
            return y, z

        y0, z0 = unit(0)
        rw = S("rcw").rearrange("p (j c) -> p j c", j=4)
        tc = [conv(XC[:, c, :], XR[:, c, :], rw, c, S("rcb")[:, c:c + 1], *txr) for c in range(4)]
        gate_t = []
        for name, dst, hb, th in (("rwa", TR, hba, tha), ("rwx", TI, hbx, thx)):
            i, ps, fr = pair()
            wv = S(name).rearrange("p (c j) -> p c j", c=4)
            for c in range(4):
                mm(ps[0:64, c * 256:(c + 1) * 256], wv[0:64, c, :], XC[0:64, c, :], True, True, fr, tc, inc=False)
                tk = mm(ps[64:128, c * 256:(c + 1) * 256], wv[64:128, c, :], XC[64:128, c, :], True, True, inc=c == 3)
            o = [act(dst[:, c, :], ps[:, c * 256:(c + 1) * 256], ACT.Tanh, tk, th, scale=0.5, bias=hb[:, c:c + 1])
                 for c in range(4)]
            freed(i, *o)
            gate_t.append(o)
        for c in range(4):
            x = ts(TR[:, c, :], TR[:, c, :], 1.0, nsp[:, c:c + 1], ADD, MUL, gate_t[0], tns)
        xa = act(AA.rearrange(flat), TR.rearrange(flat), ACT.Exp, x)
        xt = act(TR.rearrange(flat), TR.rearrange(flat), ACT.Tanh, x)
        xi = stt(TI, TI, 1.0, XC, ADD, MUL, gate_t[1], tc)
        x = tt(XC, AA, AA, MUL, xa, xi)
        x = stt(TR, XC, 1.0, TR, ADD, MUL, x, xt)
        x = act(TR.rearrange(flat), TR.rearrange(flat), ACT.Sqrt, x, scale=-1.0)
        x = stt(TI, TI, 0.5, TR, MUL, MUL, x, xi)
        for c in range(4):
            x2 = v(V.tensor_tensor_scan, (XR[:, c, :], AA[:, c, :], TI[:, c, :], 0.0, MUL, ADD), x)
        y = act(TR.rearrange(flat), GR.rearrange(flat), ACT.Square, tgr, x)
        y = ts(TR, TR, 0.044715, 1.0, MUL, ADD, y)
        y = tt(TR, TR, GR, MUL, y)
        y = act(TR.rearrange(flat), TR.rearrange(flat), ACT.Tanh, y, scale=GELU_C)
        y = stt(TR, TR, 1.0, GR, ADD, MUL, y)
        trg = stt(MT[:, 0:4, :], TR, 0.5, XR, MUL, MUL, y, x2)
        y1, z1 = unit(1, z0)
        sq = act(AA, MT[:, 4:8, :], ACT.Square, y0, y1, x2)
        r, tr = row_scales([[AA[:, h, :]] for h in range(4)], 1.0 / 128, 1e-6, 1, sq)
        i, ps, fr = pair()
        for h in range(4):
            tk = spread(ps[:, h * 256:(h + 1) * 256], r, h, 1, fr, tr, inc=h == 3)
        x = act(OO.rearrange(flat), OO.rearrange(flat), ACT.Tanh, too, scale=0.5)
        x = ts(OO, OO, 1.0, 0.5, ADD, MUL, x)
        for c in range(4):
            x = stt(OO[:, c, :], OO[:, c, :], S("mnorm")[:, c:c + 1], MT[:, 4 + c, :], MUL, MUL, x, sq)
        x = tt(MT[:, 4:8, :], OO, ps.rearrange("p (h x) -> p h x", h=4), MUL, x, tk)
        freed(i, x)
        return MT, [x, trg]

    def window(tXT):
        w = d["at_w"]
        QB, SQ, TM = take(12, 256), take(12, 256), take(4, 256)
        VV, MT = take(2, 256), take(8, 256)
        Ls = [take(4, 256) for _ in range(2)]
        Ds = [take(4, 128) for _ in range(2)]
        PTs = [take(4, 256) for _ in range(2)]
        flat = "p a b -> p (a b)"
        rc, rq = [], []
        for n in range(3):
            s, ww, t0 = load(cols(w, n * 512, 512), (8, 512))
            i, ps, tk = four_a(ww, 0, XT, 8, t0, tXT)
            release(s, tk)
            x = vcopy(QB[:, 4 * n:4 * n + 4, :].rearrange(flat), ps, tk)
            y = act(SQ[:, 4 * n:4 * n + 4, :], QB[:, 4 * n:4 * n + 4, :], ACT.Square, x)
            freed(i, x)
            rc.append(x)
            rq.append(y)
        s, ww, t0 = load(cols(w, 1536, 256), (8, 256))
        i, ps, fr = pair()
        for t in range(2):
            tk = gemm_b(ps[:, t * 256:(t + 1) * 256], ww, 0, 256, XT, t, 8, fr, t0, inc=t == 1)
        release(s, tk)
        tv = acopy(VV.rearrange(flat), ps[:, 0:512], tk)
        freed(i, tv)
        r, tr = row_scales([[SQ[:, c, :]] for c in range(12)], 1.0 / 64, 1e-6, 2, *rq)
        nsk = SC[:, 960:976]
        tsk = ts(nsk, S("sinks"), -1.0, None, MUL, None)
        tqk = []
        for n in range(3):
            q4 = QB[:, 4 * n:4 * n + 4, :]
            s4 = SQ[:, 4 * n:4 * n + 4, :]
            i, ps, fr = pair()
            for c in range(4):
                tk = spread(ps[:, c * 256:(c + 1) * 256], r, 4 * n + c, 2, fr, tr, inc=c == 3)
            gn = S("aqn") if n < 2 else S("akn")
            x = stt(q4, q4, gn, ps.rearrange("p (c x) -> p c x", c=4), MUL, MUL, tk, rc[n])
            freed(i, x)
            i, ps, fr = pair()
            for c in range(2):
                tk = mm(ps[:, c * 512:(c + 1) * 512], C("rot"), q4[:, 2 * c:2 * c + 2, :].rearrange(flat), True, True,
                        fr, x, inc=c == 1)
            y = tt(s4, ps.rearrange("p (c x) -> p c x", c=4), CS[:, 1, :].unsqueeze(1).to_broadcast([P, 4, 256]), MUL, tk, tr)
            freed(i, y)
            z = g(G.tensor_tensor, (q4, q4, CS[:, 0, :].unsqueeze(1).to_broadcast([P, 4, 256]), MUL), x, tk)
            tqk.append(tt(q4, q4, s4, ADD, y, z))

        ptr = [None, None]
        mt = []

        def start(u):
            gr, t = u // 2, u % 2
            W = P * (t + 1)
            L, D = Ls[u % 2], Ds[u % 2]
            i, ps, fr = pair()
            for j in range(4):
                h = 4 * gr + HEAD[j]
                o = 64 * (h % 2)
                c0 = (j // 2) * 512 + (j % 2) * W
                tk = mm(ps[:, c0:c0 + W], QB[o:o + 64, h // 2, t * P:(t + 1) * P], QB[o:o + 64, 8 + gr, 0:W],
                        True, True, fr, tqk, inc=j == 3)
            m = C("maskW")[:, 256 - W:256].unsqueeze(1).to_broadcast([P, 2, W])
            r, z = soft(u, L[:, :, 0:W], m, 0.125, tk, i,
                        ps.rearrange("p (b x) -> p b x", b=2)[:, :, 0:2 * W].rearrange("p b (h x) -> p b h x", h=2), W,
                        sink=(nsk[:, 4 * gr:4 * gr + 4], S("sinks")[:, 4 * gr:4 * gr + 4]))
            return [(L, D, diags(D, r, None, z))], W, t, gr, u

        def end(q):
            parts, W, t, gr, u = q
            PT = PTs[u % 2]
            x = pT(0, parts, t, PT, W, ptr[u % 2])
            i, ps, fr = pair()
            for j in range(4):
                h = HEAD[j]
                o = 64 * (h % 2)
                for kb in range(W // P):
                    tk = mm(ps[o:o + 64, (h // 2) * P:(h // 2 + 1) * P], VV[:, kb, gr * 64:(gr + 1) * 64],
                            PT[:, j, kb * P:(kb + 1) * P], kb == 0, kb == W // P - 1, fr, x, tv,
                            inc=(j == 3 and kb == W // P - 1))
            ptr[u % 2] = tk
            z = acopy(MT[:, 2 * gr:2 * gr + 2, t * P:(t + 1) * P], ps[:, 0:256].rearrange("p (h x) -> p h x", h=2), tk)
            freed(i, z)
            mt.append(z)

        prev = start(0)
        for u in range(1, 8):
            nxt = start(u)
            end(prev)
            prev = nxt
        end(prev)
        return MT, mt

    Area.at = 0
    tTz = bias_table()
    tTrig = trig()
    tXT = [tX, tTz, tTrig]
    xr = [tX]

    def finish_out(toks):
        t = pr.dma("S", s_o, out.rearrange("(t p) n -> p t n", p=P), X[:, :, :], toks)
        pr.wait("S", [t])

    stage = 0
    for l in range(2):
        tLG = load_ln(f"ln1_g{l}", f"ln1_b{l}", xr)
        state["pt"] = None
        MT, tm = mixer1(l, tXT)
        res, idx = project(MT, d[f"w_o{l}"], *tm)
        Area.at = 0

        def fsrc(tags):
            for b in (idx[0],):
                freed(b, tags[0], tags[2])
            freed(idx[1], tags[1], tags[3])
        xr, tXT = layer_norm(lambda t, h: res[(t, h)][0], lambda t, h: [res[(t, h)][1], xr], tLG,
                             S(f"g1{l}"), S(f"b1{l}"), None, fsrc)
        state["xt"] = tXT
        stage += 1
        if STOP == stage:
            return finish_out(xr)
        tLG = load_ln(f"ln2_g{l}", f"ln2_b{l}", xr)
        for k in range(4):
            hfree[k] = None
        if l == 0:
            HT, TH = take(4, 256), take(4, 256)
            y, ty = ffn(d["ffn_g"], d["ffn_u"], d["ffn_d"], 22, swiglu_hidden(HT, TH))
            Area.at = 2048 + 2048
            xr, tXT = layer_norm(lambda t, h: y[2 * t + h], lambda t, h: [ty, xr], tLG, S("g20"), S("b20"), None,
                                 add_alpha_free(y))
        else:
            xr, tXT = moe(xr, tXT, tLG)
        state["xt"] = tXT
        stage += 1
        if STOP == stage:
            return finish_out(xr)

    for l in range(2):
        Area.at = 0
        tXT = rms_in(xr, S(f"nm{l}"), tXT)
        Area.at = 0
        MT, tm = hybrid(tXT) if l == 0 else window(tXT)
        res, idx = project(MT, d[f"w_out{l}"], *tm)
        xr2 = []
        for t in range(2):
            for h in range(2):
                xs = X[:, t, h * 512:(h + 1) * 512]
                xr2.append(tt(xs, xs, res[(t, h)][0], ADD, res[(t, h)][1], xr))
        freed(idx[0], xr2[0], xr2[2])
        freed(idx[1], xr2[1], xr2[3])
        xr = xr2
        stage += 1
        if STOP == stage:
            return finish_out(xr)
        Area.at = 0
        tXT = rms_in(xr, S(f"nf{l}"), tXT)
        state["xt"] = tXT
        for k in range(4):
            hfree[k] = None
        HT, TH, CV = take(4, 256), take(4, 256), take(4, 256)
        wu = d[f"ff_up{l}"]
        y, ty = ffn(wu[:, 0:3072], wu[:, 3072:6144], d[f"ff_down{l}"], 24, conv_hidden(l, HT, TH, CV))
        xr2 = []
        for t in range(2):
            for h in range(2):
                xs = X[:, t, h * 512:(h + 1) * 512]
                xr2.append(tt(xs, xs, y[2 * t + h], ADD, ty, xr))
                free[2 * t + h] = [xr2[-1]]
        xr = xr2
        stage += 1
        if STOP == stage:
            return finish_out(xr)
        Area.at = 8192
        tXT = rms_in(xr, S(f"np{l}"), tXT)
        Area.at = 0
        TG = take(2, 1024)
        res, idx = project(XT, d[f"ple_g{l}"], *tXT)
        tg = {}
        for h in range(2):
            for t in range(2):
                tg[(t, h)] = act(TG[:, t, h * 512:(h + 1) * 512], res[(t, h)][0], ACT.Tanh, res[(t, h)][1], scale=0.5)
            freed(idx[h], tg[(0, h)], tg[(1, h)])
        sp, wp, tp = load(cols(d[f"ple_p{l}"], 0, 1024), (2, 1024))
        sq, wq, tq = load(cols(d[f"pT{l}"], 0, 256), (2, 256))
        xr2 = []
        for t in range(2):
            i, ps, fr = pair()
            for h in range(2):
                tk = gemm_b(ps[:, h * 512:(h + 1) * 512], wp, h * 512, 512, wq, t, 2, fr, tp, tq, inc=h == 1)
            x = stt(TG[:, t, :], TG[:, t, :], 1.0, ps, ADD, MUL, tk, tg[(t, 0)], tg[(t, 1)])
            freed(i, x)
            xr2.append(stt(X[:, t, :], TG[:, t, :], 0.5, X[:, t, :], MUL, ADD, x, xr))
        release(sp, tk)
        release(sq, tk)
        xr = xr2
        stage += 1
        if STOP == stage:
            return finish_out(xr)
    finish_out(xr)


def _layout(inp):
    g = {k: np.asarray(v) for k, v in inp.items()}
    x = g["x"][0]
    arr = {"x": x, "xT": x.T, "consts": const_array(), "positions": g["positions_2"][0],
           "b_v": g["hy_b_in_2"][0, 2048:2560]}
    ffn = {}
    for l in range(2):
        w = g["w_in"][l]
        kr = w[:, 640:704]
        arr[f"w_in{l}"] = np.concatenate([w[:, 0:704], kr[:, 32:64], kr[:, 0:32], w[:, 704:]], 1)
        u = g["mla_w_uq"][l].reshape(384, 4, 192)
        nope = u[:, :, 0:128].reshape(384, 512)
        rope = np.concatenate([u[:, :, 128:192], u[:, :, 160:192], u[:, :, 128:160]], 2).reshape(384, 512)
        arr[f"w_uq{l}"] = np.concatenate([nope, rope], 1)
        arr[f"w_ukv{l}"] = np.concatenate([g["mla_w_uk"][l], g["mla_w_uv"][l]], 1)
        arr[f"w_o{l}"] = g["w_o"][l]
        for n in ("ln1_g", "ln1_b", "ln2_g", "ln2_b"):
            arr[f"{n}{l}"] = g[n][l]
        arr[f"ff_up{l}"] = g["ff_w_up_2"][l]
        arr[f"ff_down{l}"] = g["ff_w_down_2"][l]
        arr[f"ple_g{l}"] = g["ple_w_gate_2"][l]
        arr[f"ple_p{l}"] = g["ple_w_proj_2"][l]
        arr[f"pT{l}"] = g["p_2"][l, 0].T
    arr["ffn_g"], arr["ffn_u"], arr["ffn_d"] = g["ffn_w_gate"][0], g["ffn_w_up"][0], g["ffn_w_down"][0]
    arr["moe_g"], arr["moe_u"], arr["moe_d"] = g["moe_w_gate"][0], g["moe_w_up"][0], g["moe_w_down"][0]
    arr["hy_w"] = g["hy_w_in_2"][0]
    arr["w_out0"], arr["w_out1"] = g["hy_w_out_2"][0], g["at_w_out_2"][0]
    q = g["at_w_qkv_2"][0]
    k4 = q[:, 1024:1280].reshape(1024, 4, 1, 64)
    arr["at_w"] = np.concatenate([q[:, 0:1024], np.concatenate([k4, k4], 2).reshape(1024, 512), q[:, 1280:1536]], 1)

    off, total = offsets(SMALLS)
    sm = np.zeros((P, total), np.float32)

    def put(name, v):
        a, n = off[name]
        sm[:v.shape[0], a:a + n] = np.reshape(v, (v.shape[0], n))

    def per(v):
        return v.reshape(-1, P).T

    for l in range(2):
        put(f"qn{l}", per(g["mla_q_norm"][l]))
        put(f"kvn{l}", per(g["mla_kv_norm"][l]))
        put(f"dn{l}", per(g["diff_norm"][l]))
        put(f"g1{l}", per(g["ln1_g"][l]))
        put(f"b1{l}", per(g["ln1_b"][l]))
        put(f"g2{l}", per(g["ln2_g"][l]))
        put(f"b2{l}", per(g["ln2_b"][l]))
        put(f"nm{l}", per(g["norm_mix_2"][l]))
        put(f"nf{l}", per(g["norm_ffn_2"][l]))
        put(f"np{l}", per(g["norm_ple_2"][l]))
        put(f"fcw{l}", g["ff_conv_w_2"][l].reshape(3, 24, P).transpose(2, 0, 1))
        put(f"fcb{l}", per(g["ff_conv_b_2"][l]))
        put(f"dl{l}", g["diff_lambda"][l].T)
    put("router", g["moe_router"][0].reshape(8, P, 8).transpose(1, 0, 2))
    put("bin", per(g["hy_b_in_2"][0, 0:3072]))
    put("bif", g["hy_b_in_2"][0, 3072:3080].reshape(2, 4).T)
    put("wif", g["hy_w_in_2"][0][:, 3072:3080].reshape(8, P, 8).transpose(1, 0, 2))
    put("rcw", g["rg_conv_w_2"][0].reshape(4, 4, P).transpose(2, 0, 1))
    put("rcb", per(g["rg_conv_b_2"][0]))
    put("rwa", g["rg_w_a_2"][0].reshape(4, P, 64).transpose(1, 0, 2))
    put("rwx", g["rg_w_x_2"][0].reshape(4, P, 64).transpose(1, 0, 2))
    put("rba", per(g["rg_b_a_2"][0]))
    put("rbx", per(g["rg_b_x_2"][0]))
    put("lam", per(g["rg_lambda_2"][0]))
    put("mcw", g["ml_conv_w_2"][0].reshape(4, 8, P).transpose(2, 0, 1))
    put("mcb", per(g["ml_conv_b_2"][0]))
    put("mnorm", per(g["ml_norm_2"][0]))
    put("aqn", np.concatenate([g["at_q_norm_2"][0]] * 2)[:, None])
    put("akn", np.concatenate([g["at_k_norm_2"][0]] * 2)[:, None])
    put("sinks", np.broadcast_to(g["at_sinks_2"][0].reshape(1, 4, 4)[:, :, HEAD], (P, 4, 4)))
    put("relb", g["rel_bias"])
    arr["smalls"] = sm
    return arr


def kernel(**inputs):
    import concourse.bacc as _bacc
    from concourse.bass_utils import run_bass_kernel_spmd as _run

    nc = _bacc.Bacc("TRN2", target_bir_lowering=False, num_devices=1)
    arrays, d = {}, {}
    for name, v in _layout(inputs).items():
        a = np.ascontiguousarray(v)
        arrays[f"in_{name}"] = a
        d[name] = nc.dram_tensor(f"in_{name}", a.shape, mybir.dt.from_np(a.dtype), kind="ExternalInput").ap()
    d["scratch"] = nc.dram_tensor("scratch", (4, 384), F, kind="Internal").ap()
    out = nc.dram_tensor("out_0", (256, 1024), F, kind="ExternalOutput").ap()
    build(nc, d, out)
    r = _run(nc, [arrays], core_ids=[0])
    return r.results[0]["out_0"].reshape(1, 256, 1024)
```

```python
import math
from contextlib import ExitStack

import numpy as np
import concourse.bass as bass
from concourse import mybir

ALU = mybir.AluOpType
ACT = mybir.ActivationFunctionType
F = mybir.dt.float32
I32 = mybir.dt.int32
FR = mybir.dt.float32r
AX = mybir.AxisListType.X
P = 128
CAP = 128
NS = 3
NU = 6
NX = 3
AREA = 14336
NEG = -1e30
ALPHA = 4 ** 0.25
HEAD = [0, 2, 1, 3]
GELU_C = math.sqrt(2.0 / math.pi)

CONSTS = [("ident", 128), ("ones", 256), ("tri", 128), ("iota", 256), ("bd2", 2), ("rot", 128), ("anti", 128), ("fold", 128),
          ("maskM", 256), ("maskW", 256), ("cos1", 256), ("oh", 384), ("sel4", 512), ("tri8", 64), ("invf", 1)]
SMALLS = [("qn0", 3), ("qn1", 3), ("kvn0", 2), ("kvn1", 2), ("dn0", 1), ("dn1", 1),
          ("g10", 8), ("g11", 8), ("b10", 8), ("b11", 8), ("g20", 8), ("g21", 8), ("b20", 8), ("b21", 8),
          ("router", 64), ("nm0", 8), ("nm1", 8), ("nf0", 8), ("nf1", 8), ("np0", 8), ("np1", 8),
          ("bin", 24), ("bif", 2), ("wif", 64), ("rcw", 16), ("rcb", 4), ("rwa", 256), ("rwx", 256), ("rba", 4), ("rbx", 4),
          ("lam", 4), ("mcw", 32), ("mcb", 8), ("mnorm", 4), ("aqn", 1), ("akn", 1), ("sinks", 16),
          ("fcw0", 72), ("fcw1", 72), ("fcb0", 24), ("fcb1", 24), ("dl0", 4), ("dl1", 4), ("relb", 4)]


def offsets(table):
    at, out = 0, {}
    for name, n in table:
        out[name] = (at, n)
        at += n
    return out, at


def const_array():
    off, total = offsets(CONSTS)
    c = np.zeros((P, total), np.float32)

    def put(name, v):
        a, n = off[name]
        v = np.asarray(v, np.float32)
        c[:v.shape[0], a:a + n] = v

    p = np.arange(P)[:, None]
    f = np.arange(P)[None, :]
    put("ident", np.eye(P))
    put("ones", np.ones((P, 256)))
    put("tri", p < f)
    put("iota", np.tile(np.arange(256), (P, 1)))
    put("bd2", np.concatenate([p < 64, p >= 64], 1))
    d = np.arange(P)
    r = np.zeros((P, P))
    for j in range(P):
        if j % 64 < 32:
            r[j + 32, j] = -1
        else:
            r[j - 32, j] = 1
    put("rot", r)
    put("anti", p + f == P - 1)
    put("fold", (p % 64) == (f % 64))
    j = np.arange(256)[None, :]
    put("maskM", np.where(j <= 128 + p, 0.0, NEG))
    put("maskW", np.where((j <= 128 + p) & (j > p), 0.0, NEG))
    pos = np.arange(256, dtype=np.float32)
    inv = (np.float32(1.0) / (np.float32(10000.0) ** (np.arange(0, 64, 2, dtype=np.float32) / np.float32(64)))).astype(np.float32)
    ang = (pos[:, None] * inv[None, :]).astype(np.float32)
    cs, sn = np.cos(ang).T, np.sin(ang).T
    put("cos1", np.concatenate([cs, cs, -sn, sn], 0))
    n = np.arange(256)
    nf = np.maximum(n, 1).astype(np.float32)
    large = 16 + (np.log(nf / np.float32(16)) / np.float32(math.log(8.0)) * np.float32(16)).astype(np.int32)
    bucket = np.where(n < 16, n, np.minimum(large, 31))
    oh = np.zeros((32, 384))
    oh[bucket, 255 - n] = 1
    put("oh", oh)
    s4 = np.zeros((4, 4, P))
    for h in range(4):
        s4[h, h] = 1
    put("sel4", s4.reshape(4, 512))
    put("tri8", np.tile((np.arange(8)[None, :] < np.arange(8)[:, None]).reshape(1, 64), (P, 1)))
    half = np.float32(10000.0) ** (-np.arange(32, dtype=np.float32) * np.float32(2.0 / 64))
    put("invf", half.astype(np.float32)[d % 32][:, None])
    return c


class Prog:

    def __init__(self, nc, ctx):
        self.nc, self.ctx = nc, ctx
        self.q = {e: [] for e in "TVAGS"}
        self.known = {e: {} for e in "TVAGS"}
        self.count = {}
        self.own = {}
        self.fresh("")

    def sem(self, name):
        s = self.ctx.enter_context(self.nc.semaphore(name))
        self.count[s] = 0
        return s

    def fresh(self, tag):
        self.own = {e: self.sem(f"done_{e}{tag}") for e in "TVAG"}

    def wait(self, e, after):
        for t in after:
            if t is None:
                continue
            if isinstance(t, list):
                self.wait(e, t)
                continue
            s, v = t
            if self.known[e].get(s, 0) < v:
                self.known[e][s] = v
                self.q[e].append(("wait", s, v))

    def op(self, e, fn, args, after, kw=None, inc=True):
        self.wait(e, after)
        s = self.own[e] if inc else None
        self.q[e].append(("op", fn, args, kw or {}, s, 1))
        if inc:
            self.count[s] += 1
            return (s, self.count[s])
        return None

    def dma(self, e, s, out, in_, after=()):
        self.wait(e, after)
        eng = {"S": self.nc.sync, "A": self.nc.scalar, "G": self.nc.gpsimd}[e]
        self.q[e].append(("op", eng.dma_start, (out, in_), {}, s, 16))
        self.count[s] += 16
        return (s, self.count[s])

    def wait_all(self, t):
        for e in "TVAGS":
            self.wait(e, [t])

    def branch(self, flag, tag):
        self.saved = (self.q, {e: dict(k) for e, k in self.known.items()}, self.own, flag)
        self.q = {e: [] for e in "TVAGS"}
        self.fresh(tag)

    def join(self):
        for e in "TVAGS":
            self.wait(e, [(s, self.count[s]) for s in self.own.values()])
        body = self.q
        self.q, self.known, self.own, flag = self.saved
        for e in "TVAGS":
            self.q[e].append(("if", flag, body[e]))

    def run(self, e, items):
        for it in items:
            if it[0] == "wait":
                self.eng[e].wait_ge(it[1], it[2])
            elif it[0] == "op":
                i = it[1](*it[2], **it[3])
                if it[4] is not None:
                    i.then_inc(it[4], it[5])
            else:
                r = self.eng[e].value_load(it[1])
                with self.eng[e].If(r == 1):
                    self.run(e, it[2])

    def flush(self):
        nc = self.nc
        self.eng = {"T": nc.tensor, "V": nc.vector, "A": nc.scalar, "G": nc.gpsimd, "S": nc.sync}
        block = self.ctx.enter_context(nc.Block())

        @block.tensor
        def _(e):
            self.run("T", self.q["T"])

        @block.vector
        def _(e):
            self.run("V", self.q["V"])

        @block.scalar
        def _(e):
            self.run("A", self.q["A"])

        @block.gpsimd
        def _(e):
            self.run("G", self.q["G"])

        @block.sync
        def _(e):
            self.run("S", self.q["S"])


def build(nc, d, out):
    plan = []
    draft = bass.Bass()
    with ExitStack() as ctx:
        program(draft, ctx, Prog(draft, ctx), d, out, None, plan)
    with ExitStack() as ctx:
        pr = Prog(nc, ctx)
        program(nc, ctx, pr, d, out, plan, [])
        pr.flush()


def program(nc, ctx, pr, d, out, plan, listed):
    def sb(name, shape, dt=F):
        return ctx.enter_context(nc.sbuf_tensor(name, shape, dt))

    V, A, G, T = nc.vector, nc.scalar, nc.gpsimd, nc.tensor

    def v(fn, args, *after, **kw):
        return pr.op("V", fn, args, after, kw)

    def a(fn, args, *after, **kw):
        return pr.op("A", fn, args, after, kw)

    def g(fn, args, *after, **kw):
        return pr.op("G", fn, args, after, kw)

    def mm(o, lhsT, rhs, start, stop, *after, inc=False, **kw):
        kw = dict(kw, start=start, stop=stop)
        return pr.op("T", T.matmul, (o, lhsT, rhs), after, kw, inc=inc)

    def act(o, i, func, *after, **kw):
        return pr.op("A", A.activation, (o, i, func), after, kw)

    def tt(o, x, y, op, *after):
        return v(V.tensor_tensor, (o, x, y, op), *after)

    def ts(o, x, s1, s2, op0, op1, *after):
        if op1 is None:
            return v(V.tensor_scalar, (o, x, s1, None, op0), *after)
        return v(V.tensor_scalar, (o, x, s1, s2, op0, op1), *after)

    def stt(o, x, s, y, op0, op1, *after):
        return v(V.scalar_tensor_tensor, (o, x, s, y, op0, op1), *after)

    def vcopy(o, i, *after):
        return v(V.tensor_copy, (o, i), *after)

    def acopy(o, i, *after):
        return act(o, i, ACT.Copy, *after)

    MUL, ADD, SUB, MAX, MIN = ALU.mult, ALU.add, ALU.subtract, ALU.max, ALU.min

    coff, cn = offsets(CONSTS)
    soff, sn = offsets(SMALLS)
    CT = sb("consts", [P, cn])
    SM = sb("smalls", [P, sn])
    X = sb("X", [P, 2, 1024])
    XT = sb("XT", [P, 8, 256])
    LG = sb("LG", [P, 2, 1024])
    RAW = sb("raw", [P, NS, 2048])
    WH = sb("wh", [P, NU, 1024], FR)
    WL = sb("wl", [P, NU, 1024], FR)
    XH = sb("xh", [P, 8, 256], FR)
    XL = sb("xl", [P, 8, 256], FR)
    YH = sb("yh", [P, 5, 256], FR)
    YL = sb("yl", [P, 5, 256], FR)
    Tz = sb("Tz", [P, 4, 256])
    CS = sb("CS", [P, 2, 256])
    SC = sb("SC", [P, 1024])
    AR = sb("arena", [P, AREA])
    PSM = ctx.enter_context(nc.psum_tensor("psum", [P, 8, 512], F))

    def C(name):
        o, n = coff[name]
        return CT[:, o:o + n]

    def S(name):
        o, n = soff[name]
        return SM[:, o:o + n]

    ident, ones = C("ident"), C("ones")[:, 0:128]

    class Area:
        at = 0

    def take(*shape):
        n = int(np.prod(shape))
        o = Area.at
        Area.at += n
        assert Area.at <= AREA, Area.at
        w = AR[:, o:o + n]
        if len(shape) == 2:
            return w.rearrange("p (a b) -> p a b", a=shape[0])
        if len(shape) == 3:
            return w.rearrange("p (a b c) -> p a b c", a=shape[0], b=shape[1])
        return w

    free = [[] for _ in range(8)]
    turn = [0]

    held = set()

    def pair(fixed=None, hold=False):
        while fixed is None and turn[0] % 4 in held:
            turn[0] += 1
        i = turn[0] % 4 if fixed is None else fixed
        if fixed is None:
            turn[0] += 1
        if hold:
            held.add(i)
        return i, PSM[:, 2 * i:2 * i + 2, :].rearrange("p a b -> p (a b)"), free[2 * i] + free[2 * i + 1]

    def freed(i, *tokens):
        held.discard(i)
        free[2 * i] = list(tokens)
        free[2 * i + 1] = list(tokens)

    lanes = [[], []]

    def pump():
        for lane in lanes:
            while lane:
                try:
                    next(lane[0])
                    break
                except StopIteration:
                    lane.pop(0)

    def drain():
        while lanes[0] or lanes[1]:
            pump()

    raws = [(RAW[:, i, :], pr.sem(f"w{i}")) for i in range(NS)]
    ring = {"raws": list(raws), "raw": [[] for _ in range(NS)], "free": [[] for _ in range(NU)], "m": 0, "n": 0, "out": 0,
            "busy": [False] * NS, "used": 0, "fetched": 0, "ready": [], "half": None}

    def split(hi, lo, x, after, flo=()):
        th = act(hi, x, ACT.Copy, *after)
        tl = tt(lo, x, hi.bitcast(F), SUB, th, *flo)
        return th, tl

    def halves(v3, by):
        _, a, b = v3.shape
        if by == "cols":
            return [v3[:, :, 0:b // 2], v3[:, :, b // 2:b]]
        return [v3[:, 0:a // 2, :], v3[:, a // 2:a, :]]

    def unit_view(w, s, shape, by):
        a, b = (shape[0], shape[1] // 2) if by == "cols" else (shape[0] // 2, shape[1])
        return w[:, s, 0:a * b].rearrange("p (a b) -> p a b", a=a)

    def fetch():
        src, shape, by = plan[ring["fetched"]]
        q = ring["m"] % len(ring["raws"])
        raw, sem = ring["raws"][q]
        ring["busy"][q] = True
        raw = raw[:, 0:shape[0] * shape[1]].rearrange("p (a b) -> p a b", a=shape[0])
        if by == "whole":
            t = pr.dma("S", sem, raw, src, ring["raw"][q])
            ring["ready"].append((("raw", q, len(ring["raws"])), raw, t))
            ring["m"] += 1
            ring["fetched"] += 1
            return
        h = 1 if ring["half"] is not None else 0
        if h == 0:
            ring["half"] = pr.dma("S", sem, raw, src, ring["raw"][q])
        s = ring["n"] % NU
        ring["n"] += 1
        ring["out"] += 1
        hi, lo = unit_view(WH, s, shape, by), unit_view(WL, s, shape, by)
        th, tl = split(hi, lo, halves(raw, by)[h], [ring["half"], ring["free"][s]])
        ring["ready"].append((s, (hi, lo), [th, tl]))
        if h == 1:
            ring["raw"][q] = [tl]
            ring["busy"][q] = False
            ring["half"] = None
            ring["m"] += 1
            ring["fetched"] += 1

    def ahead():
        while (ring["out"] < NU and ring["fetched"] < len(plan) and plan[ring["fetched"]] is not None
               and (ring["half"] is not None or not ring["busy"][ring["m"] % len(ring["raws"])])):
            fetch()

    def load(src, shape, by="cols"):
        listed.append((src, shape, by))
        if plan is None:
            if by == "whole":
                return [(0, RAW[:, 0, 0:shape[0] * shape[1]].rearrange("p (a b) -> p a b", a=shape[0]), None)]
            return [(0, (unit_view(WH, 0, shape, by), unit_view(WL, 0, shape, by)), None) for _ in range(2)]
        ahead()
        n = 1 if by == "whole" else 2
        while len(ring["ready"]) < n:
            fetch()
        ring["used"] += 1
        return [ring["ready"].pop(0) for _ in range(n)]

    def more_raws(views):
        for i, v0 in enumerate(views):
            ring["raws"].append((v0, extra_sems[i]))
            ring["raw"].append([])
            ring["busy"].append(False)
        ring["m"] = 0 if ring["half"] is None else ring["m"] % NS

    def fewer_raws():
        q = ring["m"] % len(ring["raws"])
        assert ring["half"] is None or q < NS
        ring["m"] = q if q < NS else 0
        assert not any(ring["busy"][NS:])
        del ring["raws"][NS:], ring["raw"][NS:], ring["busy"][NS:]

    extra_sems = [pr.sem(f"v{i}") for i in range(4)]

    def boundary():
        listed.append(None)
        if plan is not None:
            assert plan[ring["fetched"]] is None and not ring["ready"]
            ring["used"] += 1
            ring["fetched"] += 1

    def release(s, *tokens):
        if plan is None:
            return
        if isinstance(s, tuple):
            ring["raw"][s[1]] = list(tokens)
            ring["busy"][s[1]] = False
            return
        ring["free"][s] = list(tokens)
        ring["out"] -= 1

    def cols(w, c0, n):
        return w[:, c0:c0 + n].rearrange("(k p) n -> p k n", p=P)

    def rows(w, r0, n):
        return w[r0 * P:(r0 + n) * P, :].rearrange("(k p) n -> p k n", p=P)

    s_c, s_x, s_ln, s_o = pr.sem("c"), pr.sem("x"), pr.sem("ln"), pr.sem("o")
    tX0 = pr.dma("A", pr.sem("xt"), XT[:, :, :], d["xT"].rearrange("(k p) n -> p k n", p=P))
    pr.dma("A", s_c, CT[:, :], d["consts"])
    tC = pr.dma("A", s_c, SM[:, :], d["smalls"])
    def load_ln(gn, bn, after):
        pr.dma("A", s_ln, LG[:, 0, :], d[gn].partition_broadcast(P), after)
        return pr.dma("A", s_ln, LG[:, 1, :], d[bn].partition_broadcast(P), after)

    def rsqrt(dst, val, w, *after):
        x1, hv = w
        t = ts(x1.bitcast(I32), val.bitcast(I32), 1, None, ALU.logical_shift_right, None, *after)
        t = ts(dst.bitcast(I32), x1.bitcast(I32), -1.0, float(0x5F3759DF), MUL, ADD, t)
        t2 = ts(hv, val, -0.5, None, MUL, None, *after)
        for _ in range(3):
            t = tt(x1, dst, dst, MUL, t)
            t = tt(x1, x1, hv, MUL, t, t2)
            t = stt(dst, x1, 1.5, dst, ADD, MUL, t)
        return t

    def log1p_neg_exp(dst, x, w, *after):
        e, s, q = w
        t = ts(s, x, -1.0, None, MUL, None, *after)
        t = tt(s, x, s, MIN, t)
        t = act(e, s, ACT.Exp, t)
        t = ts(s, e, 2.0, None, ADD, None, t)
        t = v(V.reciprocal, (s, s), t)
        t = tt(s, s, e, MUL, t)
        t1 = tt(q, s, s, MUL, t)
        t = ts(dst, q, 2.0 / 19, 2.0 / 17, MUL, ADD, t1)
        for n in (15, 13, 11, 9, 7, 5, 3, 1):
            t = tt(dst, dst, q, MUL, t)
            t = ts(dst, dst, 2.0 / n, None, ADD, None, t)
        return tt(dst, dst, s, MUL, t)

    def row_scales(groups, inv_n, eps, heads, *after, at=256):
        w = len(groups) * heads
        i, ps, fr = pair()
        last = None
        for t in range(2):
            for n, chunks in enumerate(groups):
                for c, sq in enumerate(chunks):
                    o = ps[:, t * w + n * heads:t * w + (n + 1) * heads]
                    last = mm(o, sq[:, t * P:(t + 1) * P], C("bd2") if heads == 2 else ones[:, 0:1], c == 0,
                              c == len(chunks) - 1, fr, *after, inc=(t == 1 and n == len(groups) - 1 and c == len(chunks) - 1))
        val, r, w1, w2 = (SC[:, o:o + 2 * w] for o in (at, at + 2 * w, at + 4 * w, at + 6 * w))
        tk = None
        if isinstance(inv_n, list):
            pv = ps[:, 0:2 * w].rearrange("p (t n) -> p t n", t=2)
            vv = val.rearrange("p (t n) -> p t n", t=2)
            for n, (x, y) in enumerate(zip(inv_n, eps)):
                tk = ts(vv[:, :, n], pv[:, :, n], x, y, MUL, ADD, last)
        else:
            tk = ts(val, ps[:, 0:2 * w], inv_n, eps, MUL, ADD, last)
        freed(i, tk)
        tk = rsqrt(r, val, (w1, w2), tk)
        return r.rearrange("p (t n) -> p t n", t=2), tk

    def spread(ps, r, n, heads, *after, inc=True):
        tk = None
        for t in range(2):
            m = P // heads
            for h in range(heads):
                c = heads * n + h
                tk = mm(ps[h * m:(h + 1) * m, t * P:(t + 1) * P], r[:, t, c:c + 1].to_broadcast([P, m]), ident,
                        True, True, *after, inc=inc and t == 1 and h == heads - 1)
        return tk

    def gemm_a(ps, w, c0, x, kn, *after, inc=True):
        tk = None
        for k in range(kn):
            wh, wl = w[0][:, k, c0:c0 + P], w[1][:, k, c0:c0 + P]
            mm(ps, wh, x[0][:, k, :], k == 0, False, *after, XW[k] if x is XX else None)
            mm(ps, wh, x[1][:, k, :], False, False)
            tk = mm(ps, wl, x[0][:, k, :], False, k == kn - 1, inc=inc and k == kn - 1)
        return tk

    def step_b(ps, x, w, first, last, *after, inc=False):
        mm(ps, x[0], w[0], first, False, *after)
        mm(ps, x[0], w[1], False, False)
        return mm(ps, x[1], w[0], False, last, inc=inc)

    def gemm_b2(ps2, srcs, n, x, k0s, *after):
        tk = None
        total = sum(k for _, k in srcs)
        kk = 0
        for src, kn in srcs:
            for s, w, t0 in load(src, (kn, n), "rows"):
                for k in range(kn // 2):
                    for t in range(2):
                        xs = tuple(h[:, k0s + kk, t * P:(t + 1) * P] for h in x)
                        tk = step_b(ps2[t], xs, (w[0][:, k, :], w[1][:, k, :]), kk == 0, kk == total - 1, t0, *after,
                                    XW[k0s + kk] if x is XX else None,
                                    inc=k == kn // 2 - 1 and t == 1)
                    kk += 1
                release(s, tk)
                pump()
        return tk

    def four_a(w, c0, x, *after):
        i, ps, fr = pair()
        tk = None
        for c in range(2):
            for n, (s, ww, t0) in enumerate(load(cols(w, c0 + c * 256, 256), (8, 256))):
                o = ps[:, (2 * c + n) * 256:(2 * c + n + 1) * 256]
                tk = gemm_a(o, ww, 0, x, 8, fr, t0, *after)
                release(s, tk)
        return i, ps, tk

    XX, YY = (XH, XL), (YH, YL)
    XW = [[] for _ in range(8)]

    def splits(src, k0, n, *after):
        o = []
        for k in range(k0, k0 + n, 2):
            th, tl = split(XH[:, k:k + 2, :], XL[:, k:k + 2, :], src[:, k:k + 2, :], after)
            XW[k] = XW[k + 1] = [th, tl]
            o += [th, tl]
        return o

    def to_xT(Z, tz, scale, bias, *after):
        outs = []
        for b in range(2):
            i, ps, fr = pair()
            tk = None
            for t in range(2):
                for k in range(4):
                    kk = 4 * b + k
                    tk = pr.op("T", T.transpose, (ps[:, k * 256 + t * P:k * 256 + (t + 1) * P],
                                                  Z[:, t, kk * P:(kk + 1) * P], ident), (fr, tz[t]), {},
                               inc=(t == 1 and k == 3))
            tks = []
            for k in (0, 2, 1, 3):
                kk = 4 * b + k
                o, s = XT[:, kk, :], ps[:, k * 256:(k + 1) * 256]
                sc = scale[:, kk:kk + 1]
                if k < 2:
                    bb = {} if bias is None else {"bias": bias[:, kk:kk + 1]}
                    x = act(o, s, ACT.Identity if bias is not None else ACT.Copy, tk, *after, scale=sc, **bb)
                elif bias is None:
                    x = ts(o, s, sc, None, MUL, None, tk, *after)
                else:
                    x = ts(o, s, sc, bias[:, kk:kk + 1], MUL, ADD, tk, *after)
                tks.append(x)
            freed(i, *tks)
            outs += splits(XT, 4 * b, 2, tks[0], tks[2]) + splits(XT, 4 * b + 2, 2, tks[1], tks[3])
        return outs

    def layer_norm(banks, tb, gb, gT, bT, base, free_src, transposed=True):
        st = SC[:, 0:24].rearrange("p (t h s) -> p t h s", t=2, h=2)
        mv = SC[:, 24:28].rearrange("p (t s) -> p t s", t=2)
        rs, w1, w2, nb, va = (SC[:, o:o + 2] for o in (28, 30, 32, 34, 36))
        Z = take(2, 1024)
        tags, bt = [], []
        for t in range(2):
            for h in range(2):
                z = Z[:, t, h * 512:(h + 1) * 512]
                if banks is not None:
                    x = stt(z, X[:, t, h * 512:(h + 1) * 512], ALPHA, banks(t, h), MUL, ADD, tb(t, h))
                    tags.append(x)
                else:
                    z = base[:, t, h * 512:(h + 1) * 512]
                    x = tb(t, h)
                bt.append(v(V.bn_stats, (st[:, t, h, :], z), x))
        if banks is not None:
            free_src(tags)
        else:
            Z = base
        for t in range(2):
            x = v(V.bn_aggr, (mv[:, t, :], st[:, t, :, :]), *bt)
            x = ts(va[:, t:t + 1], mv[:, t, 1:2], 1e-5, None, ADD, None, x)
        x = rsqrt(rs, va, (w1, w2), x)
        x0 = v(V.scalar_tensor_tensor, (nb[:, 1:2], mv[:, 1, 0:1], -1.0, rs[:, 1:2], MUL, MUL), x)
        z1 = act(Z[:, 1, :], Z[:, 1, :], ACT.Identity, x0, scale=rs[:, 1:2], bias=nb[:, 1:2])
        z0 = ts(Z[:, 0, :], Z[:, 0, :], mv[:, 0, 0:1], rs[:, 0:1], SUB, MUL, x)
        if not transposed:
            y = []
            for t, h in ((0, 0), (0, 1), (1, 0), (1, 1)):
                c, z = slice(h * 512, (h + 1) * 512), (z0, z1)[t]
                f, op = (g, G.tensor_tensor) if (t, h) == (1, 1) else (v, V.tensor_tensor)
                u = f(op, (X[:, t, c], Z[:, t, c], LG[:, 0, c], MUL), z, gb)
                y.append(f(op, (X[:, t, c], X[:, t, c], LG[:, 1, c], ADD), u))
            return y, [z0, z1]
        tXT = to_xT(Z, [z0, z1], gT, bT)
        y = []
        for t, z in ((0, z0), (1, z1)):
            u = g(G.tensor_tensor, (X[:, t, :], Z[:, t, :], LG[:, 0, :], MUL), z, gb)
            y.append(g(G.tensor_tensor, (X[:, t, :], X[:, t, :], LG[:, 1, :], ADD), u))
        return y, tXT

    def rms_in(tx, gT, *after):
        Z = take(2, 1024)
        va, rs, w1, w2 = (SC[:, o:o + 2] for o in (42, 44, 46, 48))
        ss = SC[:, 50:54].rearrange("p (t h) -> p t h", t=2)
        tk = []
        for t in range(2):
            for h in range(2):
                c = slice(h * 512, (h + 1) * 512)
                tk.append(act(Z[:, t, c], X[:, t, c], ACT.Square, tx[(2 * t + h) if len(tx) == 4 else t], *after,
                              accum_out=ss[:, t, h:h + 1]))
        x = tt(va, ss[:, :, 0], ss[:, :, 1], ADD, *tk)
        x = ts(va, va, 1.0 / 1024, 1e-6, MUL, ADD, x)
        x = rsqrt(rs, va, (w1, w2), x)
        z0 = ts(Z[:, 0, :], X[:, 0, :], rs[:, 0:1], None, MUL, None, x)
        z1 = act(Z[:, 1, :], X[:, 1, :], ACT.Copy, x, scale=rs[:, 1:2])
        return to_xT(Z, [z0, z1], gT, None)

    def bias_table(R4, TB):
        i, ps, fr = pair()
        tk = mm(ps[0:4, 0:384], S("relb")[0:32, :], C("oh")[0:32, :], True, True, fr, tC, inc=True)
        x = vcopy(R4[0:4, :], ps[0:4, 0:384], tk)
        freed(i, x)
        s_t = pr.sem("tz")
        y = pr.dma("S", s_t, d["scratch"], R4[0:4, :], [x])
        base = d["scratch"]
        y = pr.dma("S", s_t, TB, bass.AP(tensor=base.tensor, offset=base.offset, ap=[[1, P], [384, 4], [1, 256]]), [y])
        i, ps, fr = pair()
        for n in range(2):
            tk = mm(ps[:, n * 512:(n + 1) * 512], C("anti"), TB[:, 2 * n:2 * n + 2, :].rearrange("p a b -> p (a b)"),
                    True, True, fr, y, inc=n == 1)
        x = tt(Tz[:, :, :], ps.rearrange("p (h j) -> p h j", h=4), C("maskM").unsqueeze(1).to_broadcast([P, 4, 256]),
               ADD, tk)
        freed(i, x)
        return x

    def trig(an, kk):
        x = vcopy(an, POS[:, :], tP)
        x = ts(an, an, C("invf"), None, MUL, None, x, tC)
        for n in range(2):
            rr = CS[:, n, :]
            y = ts(kk, an, 1.0 / (2 * math.pi), 0.25 if n == 0 else 0.0, MUL, ADD, x)
            y = ts(kk, kk, 12582912.0, -12582912.0, ADD, ADD, y)
            y = stt(rr, kk, -6.28125, an, MUL, ADD, y)
            y = stt(rr, kk, -0.0019340515136718750, rr, MUL, ADD, y)
            y = stt(rr, kk, -(2 * math.pi - 6.28125 - 0.0019340515136718750), rr, MUL, ADD, y)
            if n == 0:
                y = ts(rr, rr, math.pi / 2, None, ADD, None, y)
            y = ts(rr, rr, 3.1415925, -3.1415925, MIN, MAX, y)
            x = act(rr, rr, ACT.Sin, y)
        return x

    def soft(u, L, bias_ap, scale, tlog, psidx, ps, W, sink=None):
        base = 64 + 16 * (u % 8)
        nm, sm = SC[:, base:base + 4], SC[:, base + 4:base + 8]
        if sink is None:
            x = stt(L, ps, scale, bias_ap, MUL, ADD, tlog)
        else:
            for b in range(2):
                x = stt(L[:, 2 * b:2 * b + 2, :], ps[:, b], scale, bias_ap, MUL, ADD, tlog)
        freed(psidx, x)
        x = v(V.tensor_reduce, (nm, L, AX, MAX), x, negate=True)
        if sink is not None:
            x = tt(nm, nm, sink[0], MIN, x)
            sk = SC[:, base + 8:base + 12]
            y = tt(sk, nm, sink[1], ADD, x)
        tk = []
        for h in range(4):
            tk.append(act(L[:, h, :], L[:, h, :], ACT.Exp, x, bias=nm[:, h:h + 1], accum_out=sm[:, h:h + 1]))
        if sink is not None:
            z = act(sk, sk, ACT.Exp, y)
            z = tt(sm, sm, sk, ADD, z, *tk)
            tk.append(z)
        r = SC[:, base + 12:base + 16]
        z = v(V.reciprocal, (r, sm), *tk)
        return r, z

    def diags(D, r, factor, *after):
        tk = None
        for h in range(4):
            if factor is None:
                tk = ts(D[:, h, :], ident, r[:, h:h + 1], None, MUL, None, *after)
            else:
                tk = ts(D[:, h, :], ident, r[:, h:h + 1], factor, MUL, MUL, *after)
        return tk

    def pT(u, parts, t, PT, W, *after):
        i, ps, fr = pair()
        tk = None
        nb = W // P
        for h in range(4):
            for kb in range(nb):
                o = ps[:, (h * nb + kb) * P:(h * nb + kb + 1) * P]
                for n, (L, D, tl) in enumerate(parts):
                    tk = mm(o, L[:, h, kb * P:(kb + 1) * P], D[:, h, :], n == 0, n == len(parts) - 1, fr, tl,
                            inc=(h == 3 and kb == nb - 1 and n == len(parts) - 1))
        src = ps[:, 0:4 * W].rearrange("p (h x) -> p h x", h=4)
        if W == P:
            x = [vcopy(PT[:, :, 0:W], src, tk, *after)]
        else:
            x = [vcopy(PT[:, 0:2, 0:W], src[:, 0:2, :], tk, *after), acopy(PT[:, 2:4, 0:W], src[:, 2:4, :], tk, *after)]
        freed(i, *x)
        return x

    state, early = {}, {}

    def mixer1(l):
        Area.at = 0
        lam0 = 0.8 - 0.6 * math.exp(-0.3 * l)
        w = d[f"w_in{l}"]
        flat = "p a b -> p (a b)"
        QT, QR, KT, DQ, DK = take(4, 256), take(4, 256), take(4, 256), take(4, 256), take(4, 256)
        KR = take(256)
        VM, DV = take(2, 512), take(2, 512)
        CC = take(5, 256)
        MT = XT
        Ls = [take(4, 256) for _ in range(3)]
        SQ = AR[:, Area.at - 2048:Area.at - 768].rearrange("p (a b) -> p a b", a=5)
        SQ2 = Ls[0]
        Ds = [take(4, 128) for _ in range(3)]
        PTs = [take(4, 256)]
        lam = SC[:, 200:212]
        dl = S(f"dl{l}")
        x = tt(lam[0:64, 0:1], dl[0:64, 0:1], dl[0:64, 1:2], MUL, tC)
        x = tt(lam[0:64, 1:2], dl[0:64, 2:3], dl[0:64, 3:4], MUL, x)
        i0, p0, k0 = four_a(w, 0, XX)
        c0 = vcopy(CC[:, 0:4, :].rearrange(flat), p0, k0)
        q0 = act(SQ[:, 0:4, :], CC[:, 0:4, :], ACT.Square, c0)
        freed(i0, c0)
        i1, p1, k1 = four_a(w, 512, XX)
        iL, pL, fL = pair()
        kL = mm(pL[:, 0:2], C("ones")[0:64, 0:128], lam[0:64, 0:2], True, True, fL, x, inc=True)
        c1 = vcopy(CC[:, 4, :], p1[:, 0:256], k1)
        q1 = act(SQ[:, 4, :], CC[:, 4, :], ACT.Square, c1)
        KC = Ls[0][:, 0, :]
        ckr = tt(KC, p1[:, 256:512], C("cos1"), MUL, k1)
        cdq = acopy(DQ[:, 0:2, :].rearrange(flat), p1[:, 512:1024], k1)
        freed(i1, c1, ckr, cdq)
        x = act(lam[:, 2:4], pL[:, 0:2], ACT.Exp, kL)
        freed(iL, x)
        x = tt(lam[:, 4:5], lam[:, 3:4], lam[:, 2:3], SUB, x)
        tlam = ts(lam[:, 4:5], lam[:, 4:5], -lam0, None, ADD, None, x)
        nlam = lam[:, 4:5]
        N = {}

        def latent_norm():
            r, tr = row_scales([[SQ[:, c, :] for c in range(3)], [SQ[:, c, :] for c in (3, 4)]],
                               [1.0 / 384, 1.0 / 256], [1e-6, 1e-6], 1, q0, q1)
            yield
            yield
            i4, p4, f4 = pair()
            spread(p4[:, 0:256], r, 0, 1, f4, tr, inc=False)
            k4 = spread(p4[:, 256:512], r, 1, 1, tr)
            kf = mm(p4[:, 512:768], C("fold"), KC, True, True, ckr, inc=True)
            tn = []
            for c in range(5):
                sc = S(f"qn{l}")[:, c:c + 1] if c < 3 else S(f"kvn{l}")[:, c - 3:c - 2]
                rb = p4[:, 0:256] if c < 3 else p4[:, 256:512]
                tn.append(stt(CC[:, c, :], CC[:, c, :], sc, rb, MUL, MUL, k4, c0, c1, q0, q1))
            ckr2 = vcopy(KR, p4[:, 512:768], kf)
            freed(i4, tn[-1], ckr2)
            th, tl = split(YH[:, :, :], YL[:, :, :], CC, tn)
            N.update(tn=[th, tl], ckr=ckr2)

        lanes[0].append(latent_norm())
        i3, p3, f3 = pair(hold=True)
        k3 = gemm_b2([p3[:, 0:512], p3[:, 512:1024]],
                     [(w[n * 512:(n + 1) * 512, 1792:2304].rearrange("(k p) n -> p k n", p=P), 4) for n in range(2)],
                     512, XX, 0, f3)
        cdv = acopy(DV.rearrange(flat), p3, k3)
        freed(i3, cdv)
        drain()
        tn, ckr = N["tn"], N["ckr"]
        pp = []
        for n in range(2):
            i, ps, fr = pair()
            for m, (s5, w5, t5) in enumerate(load(cols(d[f"w_uq{l}"], n * 512, 512), (3, 512))):
                for c in range(2):
                    o = ps[:, (2 * m + c) * 256:(2 * m + c + 1) * 256]
                    tk = gemm_a(o, w5, c * P, YY, 3, fr, t5, tn, inc=c == 1)
                release(s5, tk)
            pp.append((i, ps, tk))
        (i6, p6, k6), (i7, p7, k7) = pp
        cq = acopy(QT.rearrange(flat), p6, k6)
        freed(i6, cq)
        cr = tt(QR, p7.rearrange("p (a b) -> p a b", a=4), C("cos1").unsqueeze(1).to_broadcast([P, 4, 256]), MUL, k7)
        freed(i7, cr)
        (s6, w6, t6), (s7, w7, t7) = load(cols(d[f"w_ukv{l}"], 0, 1024), (2, 1024))
        CK = (YH[:, 3:5, :], YL[:, 3:5, :])
        i8, p8, f8 = pair()
        for c in range(4):
            k8 = gemm_a(p8[:, c * 256:(c + 1) * 256], w6, c * P, CK, 2, f8, t6, inc=c == 3)
        release(s6, k8)
        ck = acopy(KT.rearrange(flat), p8, k8)
        freed(i8, ck)
        i9, p9, f9 = pair()
        for t in range(2):
            for k in range(2):
                k9 = step_b(p9[:, t * 512:(t + 1) * 512], tuple(h[:, k, t * P:(t + 1) * P] for h in CK),
                            (w7[0][:, k, :], w7[1][:, k, :]), k == 0, k == 1, f9, t7, inc=t == 1 and k == 1)
        release(s7, k9)
        cv = vcopy(VM.rearrange(flat), p9, k9)
        freed(i9, cv)

        def logits_mla(u, t, L, D):
            W = P * (t + 1)
            i, ps, fr = pair()
            tk = None
            for h in range(4):
                o = ps[:, h * W:(h + 1) * W]
                mm(o, QT[:, h, t * P:(t + 1) * P], KT[:, h, 0:W], True, False, fr, cq, ck)
                tk = mm(o, QR[:, h, t * P:(t + 1) * P], KR[:, 0:W], False, True, cr, ckr, inc=h == 3)
            m = C("maskM")[:, 256 - W:256].unsqueeze(1).to_broadcast([P, 4, W])
            r, z = soft(u, L[:, :, 0:W], m, (192) ** -0.5, tk, i, ps[:, 0:4 * W].rearrange("p (h x) -> p h x", h=4), W)
            return [(L, D, diags(D, r, None, z))], W, t, 0

        def logits_diff(u, t, c, L, D):
            W = P * (t + 1)
            i, ps, fr = pair()
            tk = None
            for h in range(4):
                o = ps[:, h * W:(h + 1) * W]
                tk = mm(o, DQ[64 * c:64 * c + 64, h, t * P:(t + 1) * P], DK[64 * c:64 * c + 64, h, 0:W], True, True,
                        fr, cdq, x2, y2, x5, inc=h == 3)
            r, z = soft(u, L[:, :, 0:W], Tz[:, :, 256 - W:256], 0.125, tk, i,
                        ps[:, 0:4 * W].rearrange("p (h x) -> p h x", h=4), W)
            return L, D, diags(D, r, None if c == 0 else nlam, z, tlam)

        mt = {}

        def finish(u):
            parts, W, t, base = u
            PT = PTs[0]
            x = pT(0, parts, t, PT, W, state.get("pt"))
            i, ps, fr = pair()
            tk = None
            VV = VM if base == 0 else DV
            for h in range(4):
                for kb in range(W // P):
                    tk = mm(ps[:, h * P:(h + 1) * P], VV[:, kb, h * P:(h + 1) * P], PT[:, h, kb * P:(kb + 1) * P],
                            kb == 0, kb == W // P - 1, fr, x, cv, cdv, inc=(h == 3 and kb == W // P - 1))
            state["pt"] = tk
            z = acopy(MT[:, base:base + 4, t * P:(t + 1) * P], ps[:, 0:512].rearrange("p (h x) -> p h x", h=4), tk)
            freed(i, z)
            mt[(base, t)] = z

        def latent():
            u0 = logits_mla(0, 0, Ls[0], Ds[0])
            yield
            u1 = logits_mla(1, 1, Ls[1], Ds[1])
            yield
            yield
            finish(u0)
            yield
            finish(u1)

        lanes[0].append(latent())
        if l == 0:
            bias_table(Ls[2].rearrange(flat)[:, 0:384], CC[:, 0:4, :])
        i2, p2, f2 = pair(hold=True)
        for c in range(2):
            for n, (s4, w4, t4) in enumerate(load(cols(w, 1024 + 256 * c, 256), (8, 256))):
                k2 = gemm_a(p2[:, (2 * c + n) * 256:(2 * c + n + 1) * 256], w4, 0, XX, 8, f2, t4)
                release(s4, k2)
                pump()
        x2 = acopy(DQ[:, 2:4, :].rearrange(flat), p2[:, 0:512], k2)
        y2 = vcopy(DK[:, 0:2, :].rearrange(flat), p2[:, 512:1024], k2)
        freed(i2, x2, y2)
        i5, p5, f5 = pair(hold=True)
        for n, (s4, w4, t4) in enumerate(load(cols(w, 1536, 256), (8, 256))):
            k5 = gemm_a(p5[:, n * 256:(n + 1) * 256], w4, 0, XX, 8, f5, t4)
            release(s4, k5)
            pump()
        x5 = acopy(DK[:, 2:4, :].rearrange(flat), p5[:, 0:512], k5)
        freed(i5, x5)
        drain()

        def tail():
            finish((d0, P, 0, 4))
            d1.append(logits_diff(5, 1, 1, Ls[2], Ds[2]))
            sq = [act(SQ2[:, :, 0:P], MT[:, 4:8, 0:P], ACT.Square, mt[(4, 0)])]
            yield
            yield
            finish((d1, 256, 1, 4))
            sq.append(act(SQ2[:, :, P:256], MT[:, 4:8, P:256], ACT.Square, mt[(4, 1)]))
            yield
            r, tr = row_scales([[SQ2[:, h, :]] for h in range(4)], 1.0 / 128, 1e-5, 1, sq)
            yield
            i, ps, fr = pair()
            for h in range(4):
                tk = spread(ps[:, h * 256:(h + 1) * 256], r, h, 1, fr, tr, inc=h == 3)
            dn = SC[:, 220:221]
            x = ts(dn, S(f"dn{l}"), 1.0 - lam0, None, MUL, None)
            x = stt(MT[:, 4:8, :], MT[:, 4:8, :], dn, ps.rearrange("p (h x) -> p h x", h=4), MUL, MUL, tk, x, sq)
            freed(i, x)
            splits(XT, 4, 4, x)

        splits(XT, 0, 4, mt[(0, 0)], mt[(0, 1)], k5)
        d0 = [logits_diff(2, 0, 0, Ls[2], Ds[2]), logits_diff(3, 0, 1, Ls[0], Ds[0])]
        d1 = [logits_diff(4, 1, 0, Ls[1], Ds[1])]
        lanes[0].append(tail())

    def project(w, x, kn):
        pp = [pair(hold=True), pair(hold=True)]
        fr = [p[2] for p in pp]
        tks = {}
        for g0 in range(0, kn, 2):
            units = load(rows(w, g0, 2), (2, 1024), "rows")
            last = g0 == kn - 2
            if g0 == kn // 2:
                drain()
            order = ([(k, t, h) for t in range(2) for h in range(2) for k in range(2)] if last else
                     [(k, t, h) for k in range(2) for t in range(2) for h in range(2)])
            for k, t, h in order:
                s, ww, t0 = units[k]
                kk = g0 + k
                tks[(t, h)] = step_b(pp[t][1][:, h * 512:(h + 1) * 512], tuple(q[:, kk, t * P:(t + 1) * P] for q in x),
                                     tuple(q[:, 0, h * 512:(h + 1) * 512] for q in ww), kk == 0, kk == kn - 1, t0, fr,
                                     XW[kk] if x is XX else None, inc=k == 1 if last else (t == 1 and h == 1))
                if not last and t == 1 and h == 1:
                    release(s, tks[(1, 1)])
                    pump()
            if last:
                for s, _, _ in units:
                    release(s, tks[(1, 1)])
        return {(t, h): (pp[t][1][:, h * 512:(h + 1) * 512], tks[(t, h)]) for t in range(2) for h in range(2)}, [p[0] for p in pp]

    def ffn(wg, wu, wd, nf, hidden, side=None):
        y = [PSM[:, b, :] for b in range(4)]
        yf = [list(free[b]) for b in range(4)]
        pend = []

        def down(j, hT, th):
            last = 2 * j == nf - 2
            units = load(rows(wd, 2 * j, 2), (2, 1024), "rows")
            order = [(c, b) for b in range(4) for c in range(2)] if last else [(c, b) for c in range(2) for b in range(4)]
            tks = {}
            for c, b in order:
                sd, wdv, td = units[c]
                t, h = b // 2, b % 2
                tks[b] = step_b(y[b], tuple(q[:, c * 256 + t * P:c * 256 + (t + 1) * P] for q in hT),
                                tuple(q[:, 0, h * 512:(h + 1) * 512] for q in wdv), j == 0 and c == 0,
                                2 * j + c == nf - 1, th, td, yf[b], inc=c == 1 if last else b == 3)
                if not last and b == 3:
                    release(sd, tks[3])
            if last:
                for sd, _, _ in units:
                    release(sd, tks[3])
            hfree[j % 2] = tks[3]
            return tks

        for j in range(nf // 2):
            i = 2 + j % 2
            _, ps, fr = pair(i)
            for n, wn in enumerate((wg, wu)):
                for c, (s, ww, t0) in enumerate(load(cols(wn, j * 256, 256), (8, 256))):
                    tk = gemm_a(ps[:, n * 512 + c * 256:n * 512 + (c + 1) * 256], ww, 0, XX, 8, t0, fr)
                    release(s, tk)
            pend.append((j,) + hidden(j, ps, tk, i))
            if side is not None:
                side(j)
            if len(pend) > 1:
                tq = down(*pend.pop(0))
        tq = down(*pend.pop(0))
        return y, tq

    hfree = [None] * 4
    YHf = YH[:, 0:4, :].rearrange("p a b -> p (a b)")
    YLf = YL[:, 0:4, :].rearrange("p a b -> p (a b)")

    def swiglu_hidden(HT, TH):
        def f(j, ps, tk, i):
            k = j % 2
            h, q = HT[:, k, :], TH[:, k, :]
            hh, hl = YHf[:, k * 512:(k + 1) * 512], YLf[:, k * 512:(k + 1) * 512]
            x = act(q, ps[:, 0:512], ACT.Tanh, tk, scale=0.5)
            y = stt(q, q, 1.0, ps[:, 0:512], ADD, MUL, x)
            z = stt(h, q, 0.5, ps[:, 512:1024], MUL, MUL, y)
            freed(i, z)
            th, tl = split(hh, hl, h, [z, hfree[k]])
            return (hh, hl), [th, tl]
        return f

    def conv_hidden(l, HT, TH, CV):
        fw, fb = S(f"fcw{l}").rearrange("p (j c) -> p j c", j=3), S(f"fcb{l}")

        def f(j, ps, tk, i):
            k = j % 2
            hh, hl = YHf[:, k * 512:(k + 1) * 512], YLf[:, k * 512:(k + 1) * 512]
            xs = []
            for n in range(2):
                c, gp, jj = CV[:, k, n * 256:(n + 1) * 256], ps[:, n * 256:(n + 1) * 256], 2 * j + n
                xs.append(ts(c, gp, fw[:, 2, jj:jj + 1], fb[:, jj:jj + 1], MUL, ADD, tk))
            for m in (1, 2):
                for n in range(2):
                    c, gp, jj = CV[:, k, n * 256:(n + 1) * 256], ps[:, n * 256:(n + 1) * 256], 2 * j + n
                    xs[n] = stt(c[:, m:256], gp[:, 0:256 - m], fw[:, 2 - m, jj:jj + 1], c[:, m:256], MUL, ADD, xs[n])
            c, q, h = CV[:, k, :], TH[:, k, :], HT[:, k, :]
            y = act(q, c, ACT.Square, *xs)
            y = ts(q, q, 0.044715, 1.0, MUL, ADD, y)
            y = tt(q, q, c, MUL, y)
            y = act(q, q, ACT.Tanh, y, scale=GELU_C)
            y = stt(q, q, 1.0, c, ADD, MUL, y)
            z = stt(h, q, 0.5, ps[:, 512:1024], MUL, MUL, y)
            freed(i, z)
            th, tl = split(hh, hl, h, [z, hfree[k]])
            return (hh, hl), [th, tl]
        return f

    def add_alpha_free(y):
        def fr(tags):
            for b in range(4):
                free[b] = [tags[b]]
        return fr

    def moe(xr, tXT, tLG):
        Area.at = 0
        NP = 256 // CAP
        ACC = take(2, 1024)
        XE = [take(8, CAP) for _ in range(2)]
        SE = [take(2, CAP) for _ in range(2)]
        SW = [take(2, CAP) for _ in range(2)]
        GT = [take(256) for _ in range(2)]
        YE = take(1024)
        HT = [take(2 * CAP) for _ in range(2)]
        TH = [take(2 * CAP) for _ in range(2)]
        L, pos, msk, gate, rank, s2 = (SC[:, 512 + 16 * n:528 + 16 * n] for n in range(6))
        T8 = SC[:, 608:624]
        gt = SC[:, 640:768]
        eq = SC[:, 768:896]
        sm = SC[:, 896:920]
        FL = sb("flag", [P, 8], I32)
        i, ps, fr = pair(2)
        for t in range(2):
            for k in range(8):
                tk = mm(ps[:, t * 8:(t + 1) * 8], XT[:, k, t * P:(t + 1) * P], S("router")[:, k * 8:(k + 1) * 8],
                        k == 0, k == 7, fr, tXT, inc=(t == 1 and k == 7))
        trouter = tk
        x = vcopy(L, ps[:, 0:16], tk)
        freed(2, x)
        for t in range(2):
            y = v(V.max, (T8[:, t * 8:(t + 1) * 8], L[:, t * 8:(t + 1) * 8]), x)
        Lv = L.rearrange("p (t e) -> p t e", t=2)
        g4 = gt.rearrange("p (t e j) -> p t e j", t=2, e=8)
        e4 = eq.rearrange("p (t e j) -> p t e j", t=2, e=8)
        z = None
        for t in range(2):
            lj = Lv[:, t, :].unsqueeze(1).to_broadcast([P, 8, 8])
            le = Lv[:, t, :].unsqueeze(2).to_broadcast([P, 8, 8])
            tt(g4[:, t], lj, le, ALU.is_gt, x)
            z = tt(e4[:, t], lj, le, ALU.is_equal, x)
            z = tt(e4[:, t], e4[:, t], C("tri8").rearrange("p (e j) -> p e j", e=8), MUL, z)
            z = tt(g4[:, t], g4[:, t], e4[:, t], ADD, z)
        z = v(V.tensor_reduce, (rank, gt.rearrange("p (n j) -> p n j", j=8), AX, ADD), z)
        tv = T8.rearrange("p (t e) -> p t e", t=2)
        q = tt(sm[:, 0:2], tv[:, :, 1], tv[:, :, 0], SUB, y)
        q = act(sm[:, 2:4], sm[:, 0:2], ACT.Exp, q)
        q = ts(sm[:, 4:6], sm[:, 2:4], 1.0, None, ADD, None, q)
        q = v(V.reciprocal, (sm[:, 4:6], sm[:, 4:6]), q)
        q = tt(sm[:, 6:8], sm[:, 4:6], sm[:, 2:4], MUL, q)
        s1 = ts(msk, rank, 0.0, None, ALU.is_equal, None, z)
        z2 = ts(s2, rank, 1.0, None, ALU.is_equal, None, z)
        for t in range(2):
            r = slice(t * 8, (t + 1) * 8)
            z3 = ts(gate[:, r], msk[:, r], sm[:, 4 + t:5 + t], None, MUL, None, s1, q)
            z3 = stt(gate[:, r], s2[:, r], sm[:, 6 + t:7 + t], gate[:, r], MUL, ADD, z3, z2)
        tm = tt(msk, msk, s2, ADD, z3)
        i, ps, fr = pair(2)
        mm(ps[:, 0:8], C("tri"), msk[:, 0:8], True, True, fr, tm)
        mm(ps[:, 8:16], C("tri"), msk[:, 8:16], True, False)
        mm(ps[:, 8:16], ones, msk[:, 0:8], False, True)
        mm(ps[:, 16:24], ones, msk[:, 0:8], True, False)
        tk = mm(ps[:, 16:24], ones, msk[:, 8:16], False, True, inc=True)
        tpos = vcopy(pos, ps[:, 0:16], tk)
        x = v(V.tensor_reduce, (sm[:, 8:9], ps[:, 16:24], AX, MAX), tk)
        freed(2, tpos, x)
        tfl = None
        for p in range(1, NP):
            y = ts(sm[:, 8 + p:9 + p], sm[:, 8:9], float(p * CAP), None, ALU.is_gt, None, x)
            tfl = vcopy(FL[:, p:p + 1], sm[:, 8 + p:9 + p], y)
        tacc = {0: act(ACC[:, 0, :], X[:, 0, :], ACT.Copy, xr, scale=ALPHA),
                1: act(ACC[:, 1, :], X[:, 1, :], ACT.Copy, xr, scale=ALPHA)}

        def one_pass(p):
            st = {"xe": [None, None], "gt": [None, None], "h": [None] * 4, "y": None}

            def select(e):
                b = e % 2
                o = p * CAP
                for t in range(2):
                    n = t * 8 + e
                    io = C("iota")[:, o:o + CAP]
                    x = ts(SE[b][:, t, :], io, pos[:, n:n + 1], msk[:, n:n + 1], ALU.is_equal, MUL, tpos, st["xe"][b])
                    y = ts(SW[b][:, t, :], io, pos[:, n:n + 1], gate[:, n:n + 1], ALU.is_equal, MUL, st["gt"][b])
                tsel[b] = (x, y)

            def prepare(e):
                b = e % 2
                x, y = tsel[b]
                i, ps, fr = pair(3)
                for t in range(2):
                    tk = pr.op("T", T.transpose, (ps[0:CAP, t * P:(t + 1) * P], SW[b][:, t, :], ident), (fr, y), {},
                               inc=t == 1)
                z = acopy(GT[b][0:CAP, :], ps[0:CAP, 0:256], tk, st["gt"][b])
                freed(3, z)
                tgt[b] = z
                i, ps, fr = pair(2)
                for k in range(8):
                    for t in range(2):
                        tk = mm(ps[:, k * CAP:(k + 1) * CAP], X[:, t, k * P:(k + 1) * P], SE[b][:, t, :], t == 0, t == 1,
                                fr, x, xr, inc=(k == 7 and t == 1))
                src = ps[:, 0:8 * CAP].rearrange("p (k c) -> p k c", k=8)
                txe[b] = vcopy(XE[b], src, tk, st["xe"][b])
                freed(2, txe[b])

            txe, tgt, tsel = {}, {}, {}

            def scatter(e):
                b = e % 2
                for t in range(2):
                    i, ps, fr = pair(2 + t)
                    for h in range(2):
                        tk = mm(ps[:, h * 512:(h + 1) * 512], GT[b][0:CAP, t * P:(t + 1) * P],
                                YE[0:CAP, h * 512:(h + 1) * 512], True, True, fr, tgt[b], st["ye"], inc=h == 1)
                    x = tt(ACC[:, t, :], ACC[:, t, :], ps, ADD, tk, tacc[t])
                    tacc[t] = x
                    freed(2 + t, x)
                st["gt"][b] = tk
                st["yread"] = tk

            st["yread"] = None
            select(0)
            prepare(0)
            n = 0
            for e in range(8):
                b = e % 2
                pend = []
                yf = list(free[2]) + list(free[3])

                def down(j, k, hT, th):
                    tk = None
                    for c, (sd, vd, td) in enumerate(load(rows(d["moe_d"][e], 2 * j, 2), (2, 1024), "rows")):
                        for h in range(2):
                            tk = step_b(PSM[0:CAP, 2 + h, :], tuple(q[:, c * CAP:(c + 1) * CAP] for q in hT),
                                        tuple(q[:, 0, h * 512:(h + 1) * 512] for q in vd), j == 0 and c == 0,
                                        j == 13 and c == 1, th, td, yf, inc=h == 1)
                        release(sd, tk)
                    st["h"][k] = tk
                    return tk

                for j in range(14):
                    k = n % 2
                    ps = PSM[:, k, :]
                    for m, wn in enumerate(("moe_g", "moe_u")):
                        (s, ww, t0), = load(cols(d[wn][e], j * 256, 256), (8, 256), "whole")
                        for c in range(2):
                            for q in range(8):
                                tk = mm(ps[:, (2 * m + c) * CAP:(2 * m + c + 1) * CAP], ww[:, q, c * P:(c + 1) * P],
                                        XE[b][:, q, :], q == 0, q == 7, t0, free[k], txe[b], inc=c == 1 and q == 7)
                        release(s, tk)
                    gp, up = ps[:, 0:2 * CAP], ps[:, 2 * CAP:4 * CAP]
                    x = act(TH[k], gp, ACT.Tanh, tk, scale=0.5)
                    y = stt(TH[k], TH[k], 1.0, gp, ADD, MUL, x)
                    z = stt(HT[k], TH[k], 0.5, up, MUL, MUL, y)
                    free[k] = [z]
                    hh, hl = YHf[:, k * 256:(k + 1) * 256], YLf[:, k * 256:(k + 1) * 256]
                    pend.append((j, k, (hh, hl), list(split(hh, hl, HT[k], [z, st["h"][k]]))))
                    if len(pend) > 1:
                        tq = down(*pend.pop(0))
                    n += 1
                    if j == 3 and e > 0:
                        scatter(e - 1)
                    if j == 5 and e < 7:
                        select(e + 1)
                    if j == 8 and e < 7:
                        prepare(e + 1)
                tq = down(*pend.pop(0))
                st["xe"][b] = tk
                y1 = vcopy(YE[0:CAP, 0:512], PSM[0:CAP, 2, :], tq, st["yread"])
                y2 = acopy(YE[0:CAP, 512:1024], PSM[0:CAP, 3, :], tq, st["yread"])
                st["ye"] = [y1, y2]
                free[2] = [y1]
                free[3] = [y2]
            scatter(7)

        if NX:
            more_raws([AR[:, AREA - (i + 1) * 2048:AREA - i * 2048] for i in range(NX)])
        one_pass(0)
        for p in range(1, NP):
            pr.wait_all(tfl)
            boundary()
            saved = (dict(ring, raw=list(ring["raw"]), free=list(ring["free"]), raws=list(ring["raws"]), busy=list(ring["busy"])), [list(x) for x in free], dict(tacc))
            pr.branch(FL[0:1, p:p + 1], f"_{p}")
            ring["raws"] = [(v0, pr.sem(f"w{i}_{p}")) for i, (v0, _) in enumerate(ring["raws"])]
            one_pass(p)
            pr.join()
            boundary()
            old, fr, ta = saved
            ring.update(old, used=ring["used"], fetched=ring["fetched"])
            for i in range(8):
                free[i] = fr[i]
            tacc.update(ta)
        if NX:
            fewer_raws()
        return layer_norm(None, lambda t, h: tacc[t], tLG, S("g21"), S("b21"), ACC, None, transposed=False)

    def conv(dst, src, w, c, b, *after):
        x = act(dst, src, ACT.Identity, *after, scale=w[:, 3, c:c + 1], bias=b)
        for s in range(1, 4):
            x = stt(dst[:, s:256], src[:, 0:256 - s], w[:, 3 - s, c:c + 1], dst[:, s:256], MUL, ADD, x)
        return x

    def recurrence_params():
        nsp, w1, w2, w3 = (SC[:, 976 + 4 * n:980 + 4 * n] for n in range(4))
        x = log1p_neg_exp(nsp, S("lam"), (w1, w2, w3))
        x = ts(w1, S("lam"), -1.0, 0.0, MUL, MAX, x)
        x = tt(nsp, nsp, w1, ADD, x)
        tns = ts(nsp, nsp, -4.0, None, MUL, None, x)
        hba, hbx, hmn = SC[:, 992:996], SC[:, 996:1000], SC[:, 1000:1004]
        tha = ts(hba, S("rba"), 0.5, None, MUL, None)
        thx = ts(hbx, S("rbx"), 0.5, None, MUL, None)
        thm = ts(hmn, S("mnorm"), 0.5, None, MUL, None)
        return nsp, tns, hba, tha, hbx, thx, hmn, thm

    def hybrid(tXT, params):
        nsp, tns, hba, tha, hbx, thx, hmn, thm = params
        w = d["hy_w"]
        XR, GR, QK, VV, OO = take(4, 256), take(4, 256), take(8, 256), take(2, 512), take(4, 256)
        XC, QC, MT = take(4, 256), take(8, 256), XT
        TR, TI, AA = take(4, 256), take(4, 256), take(4, 256)
        L, PT, D = QK[:, 0:4, :], QK[:, 4:8, :], take(4, 128)
        ROW = take(6, 256)
        flat = "p a b -> p (a b)"
        bn = S("bin")
        K = {}
        R = [ROW[0:4, n, :] for n in range(6)]

        def until(*names):
            while any(n not in K for n in names):
                yield

        def proj(name, dst, n0, col):
            i, ps, fr = pair(hold=True)
            for c in range(2):
                for n, (s, ww, t0) in enumerate(load(cols(w, col + c * 256, 256), (8, 256))):
                    tk = gemm_a(ps[:, (2 * c + n) * 256:(2 * c + n + 1) * 256], ww, 0, XX, 8, fr, t0)
                    release(s, tk)
                    pump()
            out = []
            for c in range(4):
                o, src, b = dst[:, c, :], ps[:, c * 256:(c + 1) * 256], bn[:, n0 + c:n0 + c + 1]
                if c >= 2:
                    out.append(act(o, src, ACT.Identity, tk, bias=b))
                else:
                    out.append(ts(o, src, b, None, ADD, None, tk))
            freed(i, *out)
            K["xx"] = tk
            K[name] = out

        def conv_silu(name, src, dst, c0, src_name):
            yield from until(src_name)
            mw = S("mcw").rearrange("p (j c) -> p j c", j=4)
            out, y = [], [None] * 4
            for c in range(5):
                if c < 4:
                    x = conv(dst[:, c, :], src[:, c, :], mw, c0 + c, S("mcb")[:, c0 + c:c0 + c + 1], *K[src_name])
                    y[c] = act(src[:, c, :], dst[:, c, :], ACT.Tanh, x, scale=0.5)
                if c > 0:
                    out.append(stt(dst[:, c - 1, :], src[:, c - 1, :], 1.0, dst[:, c - 1, :], ADD, MUL, y[c - 1]))
                if c == 4:
                    K[name] = out
                yield

        def rows_chain():
            yield from until("rows")
            ri, rf = K["rows"]
            dst, x0, (e, s, q) = R[5], R[1], (R[2], R[3], R[4])
            t = ts(s, x0, -1.0, None, MUL, None, rf)
            t = tt(s, x0, s, MIN, t)
            t = act(e, s, ACT.Exp, t)
            yield
            t = ts(s, e, 2.0, None, ADD, None, t)
            t = v(V.reciprocal, (s, s), t)
            t = tt(s, s, e, MUL, t)
            t1 = tt(q, s, s, MUL, t)
            yield
            t = ts(dst, q, 2.0 / 19, 2.0 / 17, MUL, ADD, t1)
            for n in (15, 13, 11, 9, 7, 5, 3, 1):
                t = tt(dst, dst, q, MUL, t)
                t = ts(dst, dst, 2.0 / n, None, ADD, None, t)
                if n in (13, 9, 5):
                    yield
            x = tt(dst, dst, s, MUL, t)
            x = stt(R[5], R[1], 0.0, R[5], MIN, SUB, x)
            yield
            x = v(V.tensor_tensor_scan, (R[2], C("ones")[0:4, :], R[5], 0.0, MUL, ADD), x)
            x = tt(R[0], R[0], R[2], SUB, x, ri)
            K["trow"] = x
            x = v(V.tensor_tensor_scan, (R[3], C("ones")[0:4, :], R[0], -3.0e38, MUL, MAX), x)
            tmr = tt(R[4], R[2], R[3], ADD, x)
            yield
            i, ps, fr = pair()
            for t in range(2):
                pr.op("T", T.transpose, (ps[:, t * 8:t * 8 + 4], R[3][:, t * P:(t + 1) * P], ident[0:4, 0:4]), (fr, tmr), {},
                      inc=False)
                tk = pr.op("T", T.transpose, (ps[:, t * 8 + 4:t * 8 + 8], R[4][:, t * P:(t + 1) * P], ident[0:4, 0:4]),
                           (), {}, inc=t == 1)
            K["gc"] = ts(GC, ps[:, 0:16], -1.0, None, MUL, None, tk)
            freed(i, K["gc"])
            K["em"] = act(EM, GC, ACT.Exp, K["gc"])

        GC, EM = SC[:, 540:556], SC[:, 556:572]

        def unit(t, *names):
            yield from until("trow", "gc", "em", "q", "k", *names)
            W = P * (t + 1)
            i, ps, fr = pair()
            for h in range(4):
                tk = mm(ps[:, h * W:(h + 1) * W], C("sel4")[0:4, h * P:(h + 1) * P], R[0][:, 0:W], True, True, fr,
                        K["trow"], inc=h == 3)
            Lw = L[:, :, 0:W]
            x = tt(Lw, ps[:, 0:4 * W].rearrange("p (h x) -> p h x", h=4),
                   C("maskM")[:, 256 - W:256].unsqueeze(1).to_broadcast([P, 4, W]), ADD, tk, *[K[n] for n in names])
            freed(i, x)
            ee = [act(L[:, h, 0:W], L[:, h, 0:W], ACT.Exp, x, K["gc"], bias=GC[:, t * 8 + h:t * 8 + h + 1]) for h in range(4)]
            i, ps, fr = pair(hold=True)
            for h in range(4):
                tk = mm(ps[:, h * W:(h + 1) * W], QC[:, h, t * P:(t + 1) * P], QC[:, 4 + h, 0:W], True, True, fr,
                        K["q"], K["k"], inc=h == 3)
            yield
            x = stt(Lw, ps[:, 0:4 * W].rearrange("p (h x) -> p h x", h=4), 0.25 * 128 ** -0.5, Lw, MUL, MUL, tk, *ee)
            freed(i, x)
            o = 576 + 16 * t
            dn, nd = SC[:, o:o + 4], SC[:, o + 4:o + 8]
            x = v(V.tensor_reduce, (dn, Lw, AX, ADD), x)
            x = ts(nd, dn, -1.0, None, MUL, None, x)
            x = tt(dn, dn, nd, MAX, x)
            x = tt(dn, dn, EM[:, t * 8 + 4:t * 8 + 8], MAX, x, K["em"])
            x = v(V.reciprocal, (dn, dn), x)
            x = diags(D, dn, None, x)
            yield
            z = pT(0, [(L, D, x)], t, PT, W, state.get("pt2"))
            yield
            yield from until("v")
            i, ps, fr = pair()
            for h in range(4):
                for kb in range(W // P):
                    tk = mm(ps[:, h * P:(h + 1) * P], VV[:, kb, h * P:(h + 1) * P], PT[:, h, kb * P:(kb + 1) * P],
                            kb == 0, kb == W // P - 1, fr, z, K["v"], inc=(h == 3 and kb == W // P - 1))
            state["pt2"] = tk
            y = acopy(MT[:, 4:8, t * P:(t + 1) * P], ps[:, 0:512].rearrange("p (h x) -> p h x", h=4), tk)
            freed(i, y)
            K[f"y{t}"], K[f"z{t}"] = y, z
            yield

        def merge():
            yield from until("oo", "aa")
            x = act(OO.rearrange(flat), OO.rearrange(flat), ACT.Tanh, K["oo"], scale=0.5)
            for c in range(4):
                tog = ts(OO[:, c, :], OO[:, c, :], 1.0, hmn[:, c:c + 1], ADD, MUL, x, thm)
            yield
            sq = act(AA, MT[:, 4:8, :], ACT.Square, K["y0"], K["y1"], K["aa"])
            r, tr = row_scales([[AA[:, h, :]] for h in range(4)], 1.0 / 128, 1e-6, 1, sq)
            x = tt(OO, OO, MT[:, 4:8, :], MUL, tog, K["y0"], K["y1"])
            yield
            i, ps, fr = pair()
            for h in range(4):
                tk = spread(ps[:, h * 256:(h + 1) * 256], r, h, 1, fr, tr, inc=h == 3)
            x = tt(MT[:, 4:8, :], OO, ps.rearrange("p (h x) -> p h x", h=4), MUL, x, tk, sq)
            freed(i, x)
            splits(XT, 4, 4, x, K["xx"])

        def recurrence():
            yield from until("xr")
            rw = S("rcw").rearrange("p (j c) -> p j c", j=4)
            tc = []
            for c in range(4):
                tc.append(conv(XC[:, c, :], XR[:, c, :], rw, c, S("rcb")[:, c:c + 1], *K["xr"]))
                yield
            gate_t = []
            for name, dst, hb, th in (("rwa", TR, hba, tha), ("rwx", TI, hbx, thx)):
                i, ps, fr = pair()
                wv = S(name).rearrange("p (c j) -> p c j", c=4)
                for c in range(4):
                    mm(ps[0:64, c * 256:(c + 1) * 256], wv[0:64, c, :], XC[0:64, c, :], True, True, fr, tc, inc=False)
                    tk = mm(ps[64:128, c * 256:(c + 1) * 256], wv[64:128, c, :], XC[64:128, c, :], True, True, inc=c == 3)
                o = [act(dst[:, c, :], ps[:, c * 256:(c + 1) * 256], ACT.Tanh, tk, th, scale=0.5, bias=hb[:, c:c + 1])
                     for c in range(4)]
                freed(i, *o)
                gate_t.append(o)
            yield
            for c in range(4):
                x = ts(TR[:, c, :], TR[:, c, :], 1.0, nsp[:, c:c + 1], ADD, MUL, gate_t[0], tns)
            xi = stt(TI, TI, 1.0, XC, ADD, MUL, gate_t[1], tc)
            yield from until("gr")
            y = act(AA.rearrange(flat), GR.rearrange(flat), ACT.Square, K["gr"])
            y = ts(AA, AA, 0.044715, 1.0, MUL, ADD, y)
            y = tt(AA, AA, GR, MUL, y)
            y = act(AA.rearrange(flat), AA.rearrange(flat), ACT.Tanh, y, scale=GELU_C)
            yield
            tgelu = stt(GR, AA, 1.0, GR, ADD, MUL, y)
            xa = act(AA.rearrange(flat), TR.rearrange(flat), ACT.Exp, x, tgelu)
            xt = act(TR.rearrange(flat), TR.rearrange(flat), ACT.Tanh, x)
            yield
            x = tt(XC, AA, AA, MUL, xa, xi)
            x = stt(TR, XC, 1.0, TR, ADD, MUL, x, xt)
            x = act(TR.rearrange(flat), TR.rearrange(flat), ACT.Sqrt, x, scale=-1.0)
            yield
            x = stt(TI, TI, 0.5, TR, MUL, MUL, x, xi)
            for c in range(4):
                x2 = v(V.tensor_tensor_scan, (XR[:, c, :], AA[:, c, :], TI[:, c, :], 0.0, MUL, ADD), x)
            K["aa"] = x2
            yield
            yield from until("oo")
            trg = stt(MT[:, 0:4, :], GR, 0.5, XR, MUL, MUL, tgelu, x2)
            splits(XT, 0, 4, trg, K["xx"])
            K["low"] = trg

        lanes[0] += [rows_chain(), unit(0), unit(1, "z0"), merge()]
        lanes[1] += [conv_silu("q", QK[:, 0:4, :], QC[:, 0:4, :], 0, "q0"),
                     conv_silu("k", QK[:, 4:8, :], QC[:, 4:8, :], 4, "k0"), recurrence()]
        proj("q0", QK[:, 0:4, :], 8, 1024)
        wif = S("wif").rearrange("p (k n) -> p k n", k=8)
        i, ps, fr = pair()
        for m in range(2):
            for k in range(8):
                tk = mm(ps[0:4, m * 256:(m + 1) * 256], wif[:, k, 4 * m:4 * m + 4], XT[:, k, :], k == 0, k == 7, fr, tXT,
                        inc=m == 1 and k == 7)
        ri = ts(R[0], ps[0:4, 0:256], S("bif")[0:4, 0:1], None, ADD, None, tk)
        rf = ts(R[1], ps[0:4, 256:512], S("bif")[0:4, 1:2], None, ADD, None, tk)
        freed(i, ri, rf)
        K["rows"] = (ri, rf)
        proj("k0", QK[:, 4:8, :], 12, 1536)
        proj("xr", XR, 0, 0)
        i, ps, fr = pair(hold=True)
        tk = gemm_b2([ps[:, 0:512], ps[:, 512:1024]],
                     [(w[n * 512:(n + 1) * 512, 2048:2560].rearrange("(k p) n -> p k n", p=P), 4) for n in range(2)],
                     512, XX, 0, fr)
        K["v"] = tt(VV, ps.rearrange("p (t n) -> p t n", t=2), BV[:, :].unsqueeze(1).to_broadcast([P, 2, 512]), ADD, tk, tBV)
        freed(i, K["v"])
        proj("gr", GR, 4, 512)
        proj("oo", OO, 20, 2560)
        while "low" not in K:
            pump()

    def window():
        w = d["at_w"]
        QB, SQ = take(12, 256), take(12, 256)
        VV, MT = take(2, 256), XT
        Ls = [take(4, 256) for _ in range(3)]
        Ds = [take(4, 128) for _ in range(3)]
        PTs = [take(4, 256) for _ in range(3)]
        flat = "p a b -> p (a b)"
        rc, rq, rr, tqk = {}, {}, {}, {}

        def qk(n):
            i, ps, tk = four_a(w, n * 512, XX)
            x = vcopy(QB[:, 4 * n:4 * n + 4, :].rearrange(flat), ps, tk)
            y = act(SQ[:, 4 * n:4 * n + 4, :], QB[:, 4 * n:4 * n + 4, :], ACT.Square, x)
            freed(i, x)
            rc[n], rq[n] = x, y

        def scales(n):
            rr[n] = row_scales([[SQ[:, 4 * n + c, :]] for c in range(4)], 1.0 / 64, 1e-6, 2, rq[n], at=256 + 64 * n)

        def norm(n):
            q4 = QB[:, 4 * n:4 * n + 4, :]
            i, ps, fr = pair()
            for c in range(4):
                tk = spread(ps[:, c * 256:(c + 1) * 256], rr[n][0], c, 2, fr, rr[n][1], inc=c == 3)
            gn = S("aqn") if n < 2 else S("akn")
            rc[n] = stt(q4, q4, gn, ps.rearrange("p (c x) -> p c x", c=4), MUL, MUL, tk, rc[n])
            freed(i, rc[n])

        def rope(n):
            q4, s4 = QB[:, 4 * n:4 * n + 4, :], SQ[:, 4 * n:4 * n + 4, :]
            i, ps, fr = pair()
            for c in range(2):
                tk = mm(ps[:, c * 512:(c + 1) * 512], C("rot"), q4[:, 2 * c:2 * c + 2, :].rearrange(flat), True, True,
                        fr, rc[n], inc=c == 1)
            y = tt(s4, ps.rearrange("p (c x) -> p c x", c=4), CS[:, 1, :].unsqueeze(1).to_broadcast([P, 4, 256]), MUL, tk,
                   rr[n][1], early["trig"])
            freed(i, y)
            z = tt(q4, q4, CS[:, 0, :].unsqueeze(1).to_broadcast([P, 4, 256]), MUL, rc[n], tk)
            tqk[n] = tt(q4, q4, s4, ADD, y, z)

        qk(2)
        qk(0)
        scales(2)
        i, ps, fr = pair()
        tk = gemm_b2([ps[:, 0:256], ps[:, 512:768]], [(cols(w, 1536, 256), 8)], 256, XX, 0, fr)
        tv = acopy(VV, ps.rearrange("p (t n) -> p t n", t=2)[:, :, 0:256], tk)
        freed(i, tv)
        norm(2)
        scales(0)
        nsk = SC[:, 960:976]
        tsk = ts(nsk, S("sinks"), -1.0, None, MUL, None)
        qk(1)
        rope(2)
        norm(0)
        scales(1)
        rope(0)

        ptr = [None] * 3
        mt = []

        def start(u):
            gr, t = u // 2, u % 2
            W = P * (t + 1)
            L, D = Ls[u % 3], Ds[u % 3]
            i, ps, fr = pair()
            for j in range(4):
                h = 4 * gr + HEAD[j]
                o = 64 * (h % 2)
                c0 = (j // 2) * 512 + (j % 2) * W
                tk = mm(ps[:, c0:c0 + W], QB[o:o + 64, h // 2, t * P:(t + 1) * P], QB[o:o + 64, 8 + gr, 0:W],
                        True, True, fr, tqk[gr // 2], tqk[2], inc=j == 3)
            m = C("maskW")[:, 256 - W:256].unsqueeze(1).to_broadcast([P, 2, W])
            r, z = soft(u, L[:, :, 0:W], m, 0.125, tk, i,
                        ps.rearrange("p (b x) -> p b x", b=2)[:, :, 0:2 * W].rearrange("p b (h x) -> p b h x", h=2), W,
                        sink=(nsk[:, 4 * gr:4 * gr + 4], S("sinks")[:, 4 * gr:4 * gr + 4]))
            return [(L, D, diags(D, r, None, z))], W, t, gr, u

        def turned(q):
            parts, W, t, gr, u = q
            PT = PTs[u % 3]
            return pT(0, parts, t, PT, W, ptr[u % 3])

        def end(q, x):
            parts, W, t, gr, u = q
            PT = PTs[u % 3]
            i, ps, fr = pair()
            for j in range(4):
                h = HEAD[j]
                o = 64 * (h % 2)
                for kb in range(W // P):
                    tk = mm(ps[o:o + 64, (h // 2) * P:(h // 2 + 1) * P], VV[:, kb, gr * 64:(gr + 1) * 64],
                            PT[:, j, kb * P:(kb + 1) * P], kb == 0, kb == W // P - 1, fr, x, tv,
                            inc=(j == 3 and kb == W // P - 1))
            ptr[u % 3] = tk
            z = acopy(MT[:, 2 * gr:2 * gr + 2, t * P:(t + 1) * P], ps[:, 0:256].rearrange("p (h x) -> p h x", h=2), tk)
            freed(i, z)
            mt.append(z)

        units = [start(0), start(1)]
        norm(1)
        for u in range(2, 6):
            if u == 3:
                rope(1)
            x = turned(units[u - 2])
            units.append(start(u))
            end(units[u - 2], x)
        splits(XT, 0, 4, mt[0:4])

        for u in (6, 7):
            x = turned(units[u - 2])
            units.append(start(u))
            end(units[u - 2], x)
        x6, x7 = turned(units[6]), turned(units[7])
        end(units[6], x6)
        end(units[7], x7)
        splits(XT, 4, 4, mt[4:8])

    tXT = splits(XT, 0, 4, tX0)
    if plan is not None:
        fetch()
    tXT += splits(XT, 4, 4, tX0)
    if plan is not None:
        ahead()
    tX = pr.dma("A", s_x, X[:, :, :], d["x"].rearrange("(t p) n -> p t n", p=P))
    POS = sb("pos", [P, 256], I32)
    s_p = pr.sem("p")
    tP = pr.dma("A", s_p, POS[:, :], d["positions"].partition_broadcast(P))
    BV = sb("bv", [P, 512])
    tBV = pr.dma("A", s_p, BV[:, :], d["b_v"].partition_broadcast(P))
    tP = tBV
    xr = [tX]

    def finish_out(toks):
        t = pr.dma("S", s_o, out.rearrange("(t p) n -> p t n", p=P), X[:, :, :], toks)
        pr.wait("S", [t])

    for l in range(2):
        tLG = load_ln(f"ln1_g{l}", f"ln1_b{l}", xr)
        state["pt"] = None
        mixer1(l)
        res, idx = project(d[f"w_o{l}"], XX, 8)
        Area.at = 0

        def fsrc(tags):
            freed(idx[0], tags[0], tags[1])
            freed(idx[1], tags[2], tags[3])
        xr, tXT = layer_norm(lambda t, h: res[(t, h)][0], lambda t, h: [res[(t, h)][1], xr], tLG,
                             S(f"g1{l}"), S(f"b1{l}"), None, fsrc)
        state["xt"] = tXT
        tLG = load_ln(f"ln2_g{l}", f"ln2_b{l}", xr)
        for k in range(4):
            hfree[k] = None
        if l == 0:
            HT, TH = take(2, 512), take(2, 512)
            AN, KK = take(256), take(256)

            def side(j):
                if j == 3:
                    early["params"] = recurrence_params()
                if j == 6:
                    early["trig"] = trig(AN, KK)

            y, ty = ffn(d["ffn_g"], d["ffn_u"], d["ffn_d"], 22, swiglu_hidden(HT, TH), side)
            Area.at = 2048 + 2048
            xr, tXT = layer_norm(lambda t, h: y[2 * t + h], lambda t, h: [ty[2 * t + h], xr], tLG, S("g20"), S("b20"), None,
                                 add_alpha_free(y))
        else:
            xr, tXT = moe(xr, tXT, tLG)
        state["xt"] = tXT

    for l in range(2):
        Area.at = 0
        tXT = rms_in(xr, S(f"nm{l}"), tXT)
        Area.at = 0
        if l == 0:
            hybrid(tXT, early["params"])
        else:
            window()
        res, idx = project(d[f"w_out{l}"], XX, 8)
        xr2 = []
        for t in range(2):
            for h in range(2):
                xs = X[:, t, h * 512:(h + 1) * 512]
                xr2.append(tt(xs, xs, res[(t, h)][0], ADD, res[(t, h)][1], xr))
        freed(idx[0], xr2[0], xr2[1])
        freed(idx[1], xr2[2], xr2[3])
        xr = xr2
        Area.at = 0
        tXT = rms_in(xr, S(f"nf{l}"), tXT)
        state["xt"] = tXT
        for k in range(4):
            hfree[k] = None
        HT, TH, CV = take(2, 512), take(2, 512), take(2, 512)
        wu = d[f"ff_up{l}"]
        y, ty = ffn(wu[:, 0:3072], wu[:, 3072:6144], d[f"ff_down{l}"], 24, conv_hidden(l, HT, TH, CV))
        xr2 = []
        for t in range(2):
            for h in range(2):
                xs = X[:, t, h * 512:(h + 1) * 512]
                xr2.append(tt(xs, xs, y[2 * t + h], ADD, ty[2 * t + h], xr))
                free[2 * t + h] = [xr2[-1]]
        xr = xr2
        Area.at = 8192
        tXT = rms_in(xr, S(f"np{l}"), tXT)
        Area.at = 0
        TG = take(2, 1024)
        res, idx = project(d[f"ple_g{l}"], XX, 8)
        tg = {}
        for h in range(2):
            for t in range(2):
                tg[(t, h)] = act(TG[:, t, h * 512:(h + 1) * 512], res[(t, h)][0], ACT.Tanh, res[(t, h)][1], scale=0.5)
        for t in range(2):
            freed(idx[t], tg[(t, 0)], tg[(t, 1)])
        uq = load(cols(d[f"pT{l}"], 0, 256), (2, 256))
        up = load(cols(d[f"ple_p{l}"], 0, 1024), (2, 1024))
        xr2 = []
        for t in range(2):
            i, ps, fr = pair()
            for h in range(2):
                for k in range(2):
                    tk = step_b(ps[:, h * 512:(h + 1) * 512], tuple(q[:, k, :] for q in uq[t][1]),
                                tuple(q[:, k, :] for q in up[h][1]), k == 0, k == 1, fr, uq[t][2], up[h][2],
                                inc=h == 1 and k == 1)
            x = stt(TG[:, t, :], TG[:, t, :], 1.0, ps, ADD, MUL, tk, tg[(t, 0)], tg[(t, 1)])
            freed(i, x)
            xr2.append(stt(X[:, t, :], TG[:, t, :], 0.5, X[:, t, :], MUL, ADD, x, xr))
        for q in uq + up:
            release(q[0], tk)
        xr = xr2
    finish_out(xr)


def _layout(inp):
    g = {k: np.asarray(v) for k, v in inp.items()}
    x = g["x"][0]
    arr = {"x": x, "xT": x.T, "consts": const_array(), "positions": g["positions_2"][0],
           "b_v": g["hy_b_in_2"][0, 2048:2560]}
    ffn = {}
    for l in range(2):
        w = g["w_in"][l]
        kr = w[:, 640:704]
        arr[f"w_in{l}"] = np.concatenate([w[:, 0:704], kr[:, 32:64], kr[:, 0:32], w[:, 704:]], 1)
        u = g["mla_w_uq"][l].reshape(384, 4, 192)
        nope = u[:, :, 0:128].reshape(384, 512)
        rope = np.concatenate([u[:, :, 128:192], u[:, :, 160:192], u[:, :, 128:160]], 2).reshape(384, 512)
        arr[f"w_uq{l}"] = np.concatenate([nope, rope], 1)
        arr[f"w_ukv{l}"] = np.concatenate([g["mla_w_uk"][l], g["mla_w_uv"][l]], 1)
        arr[f"w_o{l}"] = g["w_o"][l]
        for n in ("ln1_g", "ln1_b", "ln2_g", "ln2_b"):
            arr[f"{n}{l}"] = g[n][l]
        arr[f"ff_up{l}"] = g["ff_w_up_2"][l]
        arr[f"ff_down{l}"] = g["ff_w_down_2"][l]
        arr[f"ple_g{l}"] = g["ple_w_gate_2"][l]
        arr[f"ple_p{l}"] = g["ple_w_proj_2"][l]
        arr[f"pT{l}"] = g["p_2"][l, 0].T
    arr["ffn_g"], arr["ffn_u"], arr["ffn_d"] = g["ffn_w_gate"][0], g["ffn_w_up"][0], g["ffn_w_down"][0]
    arr["moe_g"], arr["moe_u"], arr["moe_d"] = g["moe_w_gate"][0], g["moe_w_up"][0], g["moe_w_down"][0]
    arr["hy_w"] = g["hy_w_in_2"][0]
    arr["w_out0"], arr["w_out1"] = g["hy_w_out_2"][0], g["at_w_out_2"][0]
    q = g["at_w_qkv_2"][0]
    k4 = q[:, 1024:1280].reshape(1024, 4, 1, 64)
    arr["at_w"] = np.concatenate([q[:, 0:1024], np.concatenate([k4, k4], 2).reshape(1024, 512), q[:, 1280:1536]], 1)

    off, total = offsets(SMALLS)
    sm = np.zeros((P, total), np.float32)

    def put(name, v):
        a, n = off[name]
        sm[:v.shape[0], a:a + n] = np.reshape(v, (v.shape[0], n))

    def per(v):
        return v.reshape(-1, P).T

    for l in range(2):
        put(f"qn{l}", per(g["mla_q_norm"][l]))
        put(f"kvn{l}", per(g["mla_kv_norm"][l]))
        put(f"dn{l}", per(g["diff_norm"][l]))
        put(f"g1{l}", per(g["ln1_g"][l]))
        put(f"b1{l}", per(g["ln1_b"][l]))
        put(f"g2{l}", per(g["ln2_g"][l]))
        put(f"b2{l}", per(g["ln2_b"][l]))
        put(f"nm{l}", per(g["norm_mix_2"][l]))
        put(f"nf{l}", per(g["norm_ffn_2"][l]))
        put(f"np{l}", per(g["norm_ple_2"][l]))
        put(f"fcw{l}", g["ff_conv_w_2"][l].reshape(3, 24, P).transpose(2, 0, 1))
        put(f"fcb{l}", per(g["ff_conv_b_2"][l]))
        put(f"dl{l}", g["diff_lambda"][l].T)
    put("router", g["moe_router"][0].reshape(8, P, 8).transpose(1, 0, 2))
    put("bin", per(g["hy_b_in_2"][0, 0:3072]))
    put("bif", g["hy_b_in_2"][0, 3072:3080].reshape(2, 4).T)
    put("wif", g["hy_w_in_2"][0][:, 3072:3080].reshape(8, P, 8).transpose(1, 0, 2))
    put("rcw", g["rg_conv_w_2"][0].reshape(4, 4, P).transpose(2, 0, 1))
    put("rcb", per(g["rg_conv_b_2"][0]))
    put("rwa", g["rg_w_a_2"][0].reshape(4, P, 64).transpose(1, 0, 2))
    put("rwx", g["rg_w_x_2"][0].reshape(4, P, 64).transpose(1, 0, 2))
    put("rba", per(g["rg_b_a_2"][0]))
    put("rbx", per(g["rg_b_x_2"][0]))
    put("lam", per(g["rg_lambda_2"][0]))
    put("mcw", g["ml_conv_w_2"][0].reshape(4, 8, P).transpose(2, 0, 1))
    put("mcb", per(g["ml_conv_b_2"][0]))
    put("mnorm", per(g["ml_norm_2"][0]))
    put("aqn", np.concatenate([g["at_q_norm_2"][0]] * 2)[:, None])
    put("akn", np.concatenate([g["at_k_norm_2"][0]] * 2)[:, None])
    put("sinks", np.broadcast_to(g["at_sinks_2"][0].reshape(1, 4, 4)[:, :, HEAD], (P, 4, 4)))
    put("relb", g["rel_bias"])
    arr["smalls"] = sm
    return arr


def kernel(**inputs):
    import concourse.bacc as _bacc
    from concourse.bass_utils import run_bass_kernel_spmd as _run

    nc = _bacc.Bacc("TRN2", target_bir_lowering=False, num_devices=1)
    arrays, d = {}, {}
    for name, v in _layout(inputs).items():
        a = np.ascontiguousarray(v)
        arrays[f"in_{name}"] = a
        d[name] = nc.dram_tensor(f"in_{name}", a.shape, mybir.dt.from_np(a.dtype), kind="ExternalInput").ap()
    d["scratch"] = nc.dram_tensor("scratch", (4, 384), F, kind="Internal").ap()
    out = nc.dram_tensor("out_0", (256, 1024), F, kind="ExternalOutput").ap()
    build(nc, d, out)
    r = _run(nc, [arrays], core_ids=[0])
    return r.results[0]["out_0"].reshape(1, 256, 1024)
```
